# Optimizing a Trainium2 kernel written in Bass

```python
import math
import jax, jax.numpy as jnp
from jax import lax
import numpy as np

D_MODEL = 1024
BATCH = 1
SEQ = 512
DEPTH = 2

EPS = 1e-6
D_FF = 2816

RET_HEADS = 4
RET_DK = 128
RET_DV = 256
RET_QK = RET_HEADS * RET_DK
RET_V = RET_HEADS * RET_DV
RET_CHUNK = 128
ROPE_BASE = 10000.0

DIL_CONFIGS = ((128, 1), (512, 4), (2048, 16))
DIL_HEADS_PER_GROUP = 4
DIL_HEADS = DIL_HEADS_PER_GROUP * len(DIL_CONFIGS)
DIL_DH = 128
DIL_WIDTH = DIL_HEADS * DIL_DH
DIL_OUT = DIL_HEADS_PER_GROUP * DIL_DH
N_BUCKETS = 32
MAX_DISTANCE = 1024
NEG = -1e30

IN_SIZES = (RET_QK, RET_QK, RET_V, RET_V, DIL_WIDTH, DIL_WIDTH, DIL_WIDTH, D_MODEL, D_MODEL)
IN_WIDTH = sum(IN_SIZES)
IN_SPLITS = tuple(int(s) for s in np.cumsum(IN_SIZES)[:-1])

kernel_name = "hybrid_retention_dilated_macaron_encoder"

def rmsnorm(x, g):
    x32 = x.astype(jnp.float32)
    r = lax.rsqrt(jnp.mean(x32 * x32, axis=-1, keepdims=True) + EPS)
    return (x32 * r * g).astype(x.dtype)

def swiglu(h, w_gate, w_up, w_down):
    return (jax.nn.silu(h @ w_gate) * (h @ w_up)) @ w_down

def rope(t, pos):
    half = t.shape[-1] // 2
    inv = ROPE_BASE ** (-jnp.arange(half, dtype=jnp.float32) / half)
    ang = pos[:, None] * inv[None, :]
    cos, sin = jnp.cos(ang), jnp.sin(ang)
    t1, t2 = t[..., :half], t[..., half:]
    return jnp.concatenate([t1 * cos - t2 * sin, t1 * sin + t2 * cos], axis=-1)

def _retention_dir(q, k, v, log_gamma, strict):
    B, H, S, dk = q.shape
    dv = v.shape[-1]
    C = RET_CHUNK
    N = S // C
    qc = q.reshape(B, H, N, C, dk)
    kc = k.reshape(B, H, N, C, dk)
    vc = v.reshape(B, H, N, C, dv)
    idx = jnp.arange(C, dtype=jnp.float32)
    diff = idx[:, None] - idx[None, :]
    mask = (diff > 0) if strict else (diff >= 0)
    lg = log_gamma[:, None, None]
    dmat = jnp.where(mask[None], jnp.exp(lg * jnp.maximum(diff, 0.0)[None]), 0.0)
    scores = jnp.einsum('bhncd,bhnjd->bhncj', qc, kc) * dmat[None, :, None]
    o_inner = jnp.einsum('bhncj,bhnje->bhnce', scores, vc)
    q_decay = jnp.exp(log_gamma[:, None] * (idx + 1.0)[None])
    k_decay = jnp.exp(log_gamma[:, None] * (C - 1.0 - idx)[None])
    chunk_decay = jnp.exp(log_gamma * C)

    def step(state, xs):
        qn, kn, vn = xs
        cross = jnp.einsum('bhcd,bhde->bhce', qn * q_decay[None, :, :, None], state)
        state = state * chunk_decay[None, :, None, None] + jnp.einsum(
            'bhcd,bhce->bhde', kn * k_decay[None, :, :, None], vn)
        return state, cross

    xs = (jnp.moveaxis(qc, 2, 0), jnp.moveaxis(kc, 2, 0), jnp.moveaxis(vc, 2, 0))
    state0 = jnp.zeros((B, H, dk, dv), jnp.float32)
    _, cross = lax.scan(step, state0, xs)
    out = o_inner + jnp.moveaxis(cross, 0, 2)
    return out.reshape(B, H, S, dv)

def retention(q, k, v, g, decay_exp, norm_g):
    B, S, _ = q.shape
    dtype = q.dtype
    pos = jnp.arange(S, dtype=jnp.float32)
    heads = lambda t, d: t.astype(jnp.float32).reshape(B, S, RET_HEADS, d).transpose(0, 2, 1, 3)
    qh = rope(heads(q, RET_DK), pos)
    kh = rope(heads(k, RET_DK), pos) * (RET_DK ** -0.5)
    vh = heads(v, RET_DV)
    log_gamma = jnp.log1p(-jnp.exp2(-decay_exp.astype(jnp.float32)))
    fwd = _retention_dir(qh, kh, vh, log_gamma[0], strict=False)
    flip = lambda t: jnp.flip(t, axis=2)
    bwd = flip(_retention_dir(flip(qh), flip(kh), flip(vh), log_gamma[1], strict=True))
    o = fwd + bwd
    o = o * lax.rsqrt(jnp.mean(o * o, axis=-1, keepdims=True) + EPS)
    o = o.transpose(0, 2, 1, 3).reshape(B, S, RET_V) * norm_g
    return (jax.nn.silu(g.astype(jnp.float32)) * o).astype(dtype)

def t5_bucket(rel):
    nb = N_BUCKETS // 2
    max_exact = nb // 2
    ret = jnp.where(rel > 0, nb, 0)
    n = jnp.abs(rel)
    nf = jnp.maximum(n, 1).astype(jnp.float32)
    large = max_exact + (jnp.log(nf / max_exact) / math.log(MAX_DISTANCE / max_exact)
                         * (nb - max_exact)).astype(jnp.int32)
    large = jnp.minimum(large, nb - 1)
    return ret + jnp.where(n < max_exact, n, large)

def _dilated_group(q, k, v, bias, d, R):
    B, Hg, S, dh = q.shape
    L = S // d
    nb = -(-L // R)
    Lp = nb * R

    def by_residue(t):
        t = t.reshape(B, Hg, L, d, dh).transpose(0, 1, 3, 2, 4)
        return jnp.pad(t, ((0, 0), (0, 0), (0, 0), (0, Lp - L), (0, 0)))

    def windows(t):
        t = jnp.pad(by_residue(t), ((0, 0), (0, 0), (0, 0), (R, R), (0, 0)))
        t = t.reshape(B, Hg, d, nb + 2, R, dh)
        return jnp.concatenate([t[:, :, :, 0:nb], t[:, :, :, 1:nb + 1], t[:, :, :, 2:nb + 2]], axis=-2)

    qs = by_residue(q).reshape(B, Hg, d, nb, R, dh)
    kw = windows(k)
    vw = windows(v).astype(jnp.float32)
    n_i = jnp.arange(nb)[:, None, None]
    a_i = jnp.arange(R)[None, :, None]
    c_i = jnp.arange(3 * R)[None, None, :]
    j_abs = (n_i - 1) * R + c_i
    valid = (j_abs >= 0) & (j_abs < L) & (jnp.abs(c_i - R - a_i) <= R)
    s = jnp.einsum('bhrnid,bhrnjd->bhrnij', qs, kw).astype(jnp.float32) + bias[None, :, None, None]
    s = jnp.where(valid[None, None, None], s, NEG)
    m = jnp.max(s, axis=-1, keepdims=True)
    p = jnp.exp(s - m)
    den = jnp.sum(p, axis=-1)
    o = jnp.einsum('bhrnij,bhrnjd->bhrnid', p, vw) / den[..., None]
    lse = m[..., 0] + jnp.log(den)
    o = o.reshape(B, Hg, d, Lp, dh)[:, :, :, :L].transpose(0, 1, 3, 2, 4).reshape(B, Hg, S, dh)
    lse = lse.reshape(B, Hg, d, Lp)[..., :L].transpose(0, 1, 3, 2).reshape(B, Hg, S)
    return o, lse

def dilated_attention(q, k, v, q_norm, k_norm, rel_bias):
    B, S, _ = q.shape
    dtype = q.dtype
    heads = lambda t: t.reshape(B, S, DIL_HEADS, DIL_DH).transpose(0, 2, 1, 3)
    qh = rmsnorm(heads(q), q_norm) * (DIL_DH ** -0.5)
    kh = rmsnorm(heads(k), k_norm)
    vh = heads(v)
    outs, lses = [], []
    for gi, (window, d) in enumerate(DIL_CONFIGS):
        R = window // (2 * d)
        sl = slice(gi * DIL_HEADS_PER_GROUP, (gi + 1) * DIL_HEADS_PER_GROUP)
        a_i = jnp.arange(R)[:, None]
        c_i = jnp.arange(3 * R)[None, :]
        bucket = t5_bucket((c_i - R - a_i) * d)
        bias = rel_bias[bucket][..., sl].transpose(2, 0, 1).astype(jnp.float32)
        o, lse = _dilated_group(qh[:, sl], kh[:, sl], vh[:, sl], bias, d, R)
        outs.append(o)
        lses.append(lse)
    w = jax.nn.softmax(jnp.stack(lses, axis=0), axis=0)
    out = jnp.sum(w[..., None] * jnp.stack(outs, axis=0), axis=0)
    return out.transpose(0, 2, 1, 3).reshape(B, S, DIL_OUT).astype(dtype)

def setup_inputs(seed: int = 0) -> dict:
    key = jax.random.key(seed)
    ks = jax.random.split(key, 24)
    f32 = jnp.float32
    nrm = lambda k, shape, fan_in: jax.random.normal(k, shape, f32) * (fan_in ** -0.5)
    gain = lambda k, shape: 1.0 + 0.02 * jax.random.normal(k, shape, f32)
    decay_exp = (5.0 + jnp.arange(RET_HEADS, dtype=f32))[None, None, :] + \
        0.25 * jax.random.uniform(ks[9], (DEPTH, 2, RET_HEADS), f32)
    return {
        "x": jax.random.normal(ks[0], (BATCH, SEQ, D_MODEL), f32),
        "rel_bias": 0.2 * jax.random.normal(ks[1], (N_BUCKETS, DIL_HEADS), f32),
        "norm_ffn1": gain(ks[2], (DEPTH, D_MODEL)),
        "ffn1_gate": nrm(ks[3], (DEPTH, D_MODEL, D_FF), D_MODEL),
        "ffn1_up": nrm(ks[4], (DEPTH, D_MODEL, D_FF), D_MODEL),
        "ffn1_down": nrm(ks[5], (DEPTH, D_FF, D_MODEL), D_FF),
        "norm_mix": gain(ks[6], (DEPTH, D_MODEL)),
        "w_in": nrm(ks[7], (DEPTH, D_MODEL, IN_WIDTH), D_MODEL),
        "b_gate": 0.02 * jax.random.normal(ks[8], (DEPTH, 2 * D_MODEL), f32),
        "ret_decay_exp": decay_exp,
        "ret_norm": gain(ks[10], (DEPTH, RET_V)),
        "w_ret_o": nrm(ks[11], (DEPTH, RET_V, D_MODEL), RET_V),
        "dil_q_norm": gain(ks[12], (DEPTH, DIL_DH)),
        "dil_k_norm": gain(ks[13], (DEPTH, DIL_DH)),
        "w_dil_o": nrm(ks[14], (DEPTH, DIL_OUT, D_MODEL), DIL_OUT),
        "w_out": nrm(ks[15], (DEPTH, D_MODEL, D_MODEL), D_MODEL),
        "norm_ffn2": gain(ks[16], (DEPTH, D_MODEL)),
        "ffn2_gate": nrm(ks[17], (DEPTH, D_MODEL, D_FF), D_MODEL),
        "ffn2_up": nrm(ks[18], (DEPTH, D_MODEL, D_FF), D_MODEL),
        "ffn2_down": nrm(ks[19], (DEPTH, D_FF, D_MODEL), D_FF),
    }

def reference(x, rel_bias, norm_ffn1, ffn1_gate, ffn1_up, ffn1_down, norm_mix, w_in,
              b_gate, ret_decay_exp, ret_norm, w_ret_o, dil_q_norm, dil_k_norm, w_dil_o,
              w_out, norm_ffn2, ffn2_gate, ffn2_up, ffn2_down):
    for l in range(DEPTH):
        x = x + 0.5 * swiglu(rmsnorm(x, norm_ffn1[l]), ffn1_gate[l], ffn1_up[l], ffn1_down[l])
        h = rmsnorm(x, norm_mix[l])
        z = h @ w_in[l]
        rq, rk, rv, rg, dq, dk, dv, g_ret, g_dil = jnp.split(z, IN_SPLITS, axis=-1)
        y_ret = retention(rq, rk, rv, rg, ret_decay_exp[l], ret_norm[l]) @ w_ret_o[l]
        y_dil = dilated_attention(dq, dk, dv, dil_q_norm[l], dil_k_norm[l], rel_bias) @ w_dil_o[l]
        gates = jax.nn.sigmoid(jnp.concatenate([g_ret, g_dil], axis=-1) + b_gate[l])
        merged = gates[..., :D_MODEL] * y_ret + gates[..., D_MODEL:] * y_dil
        x = x + merged @ w_out[l]
        x = x + 0.5 * swiglu(rmsnorm(x, norm_ffn2[l]), ffn2_gate[l], ffn2_up[l], ffn2_down[l])
    return x


_drawn_inputs = setup_inputs


def setup_inputs(seed=0):
    import zlib

    import numpy as np

    out = dict(_drawn_inputs(seed))
    spreads = {}
    factors = {'rel_bias': 3.463,
     'norm_ffn1': 3.932,
     'norm_mix': 2.862,
     'b_gate': 8.0,
     'ret_norm': 6.281,
     'dil_q_norm': 8.0,
     'dil_k_norm': 8.0,
     'norm_ffn2': 5.128}
    for name, (base, spread) in spreads.items():
        noise = np.random.default_rng([zlib.crc32(name.encode()), seed]).standard_normal(out[name].shape)
        drawn = base * np.exp(spread * noise) if base else spread * noise
        out[name] = __import__('jax').numpy.asarray(drawn.astype(out[name].dtype))
    for name, factor in factors.items():
        out[name] = (out[name] * factor).astype(out[name].dtype)
    return out
```

```python
import math
from typing import NamedTuple

import numpy as np
import concourse.bass as bass
from concourse import mybir
from contextlib import ExitStack

P = 128
SEQ, D_MODEL, DEPTH, D_FF = 512, 1024, 2, 2816
RET_HEADS, RET_DK, RET_DV = 4, 128, 256
DIL_GROUPS, DIL_HPG, DIL_DH = 3, 4, 128
N_BUCKETS, MAX_DISTANCE, EPS, NEG = 32, 1024, 1e-6, -1e30
KT = D_MODEL // P
NB = SEQ // P
C_RQ, C_RK, C_RV, C_RG = 0, 512, 1024, 2048
C_DQ, C_DK, C_DV, C_GR, C_GD = 3072, 4608, 6144, 7680, 8704
GRP = 256
GROUPS = D_FF // GRP
PAIRS = (GROUPS - 1) // 2
NC, NT, WD = 2 * NB - 1, 2 * NB + 1, 2 * P
R_N = (0, 8, 16)
R_BG, R_RN, R_QN, R_KN, ROWS = 24, 40, 48, 49, 50


class Unit(NamedTuple):
    index: object
    slot: int
    turn: object
    tile: object
    before: int


FFN_TILES = [2, 2] + [8, 2, 2] * (GROUPS - 1) + [8]
HEAD_TILES = [2, 4, 2, 2, 2, 2, 1, 4]
MERGE_TILES = [2, 2] + [8, 2, 2] * (KT - 1) + [8]
TILES = FFN_TILES + HEAD_TILES * RET_HEADS + MERGE_TILES + FFN_TILES
FFN_BASE = (0, len(FFN_TILES) + len(HEAD_TILES) * RET_HEADS + len(MERGE_TILES))
HEAD_BASE = len(FFN_TILES)
MERGE_BASE = HEAD_BASE + len(HEAD_TILES) * RET_HEADS
UNITS_LAYER, TILES_LAYER = len(TILES), sum(TILES)
FIRST_CREDIT = 9
FREE = 1
LO_CREDIT = 2


def unit(layer, fixed, loop=0, loop_units=0, loop_tiles=0):
    return Unit(layer * UNITS_LAYER + loop * loop_units + fixed, fixed % 2,
                layer * (UNITS_LAYER // 2) + loop * (loop_units // 2) + fixed // 2,
                layer * TILES_LAYER + loop * loop_tiles + sum(TILES[:fixed]), TILES[fixed - 1])


def build(nc, x, rel_bias, norm_ffn1, ffn1_gate, ffn1_up, ffn1_down, norm_mix, w_in, b_gate, ret_decay_exp,
          ret_norm, w_ret_o, dil_q_norm, dil_k_norm, w_dil_o, w_out, norm_ffn2, ffn2_gate, ffn2_up, ffn2_down,
          c_ident, c_cos, c_sin, c_onehot, c_dist, c_sel, out):
    fp32, f32r = mybir.dt.float32, mybir.dt.float32r
    ALU, ACT, AX = mybir.AluOpType, mybir.ActivationFunctionType, mybir.AxisListType
    ds = bass.ds

    x_spill = nc.dram_tensor("x_spill", [P, KT, SEQ], fp32, kind="Internal").ap()
    bias_diag = nc.dram_tensor("bias_diag", [DIL_GROUPS * DIL_HPG, NT * WD], fp32, kind="Internal")
    bias_full = nc.dram_tensor("bias_full", [P, DIL_HPG, NT, P], fp32, kind="Internal").ap()
    decay_diag = nc.dram_tensor("decay_diag", [DEPTH * RET_HEADS * NC, WD], fp32, kind="Internal")
    decay_full = nc.dram_tensor("decay_full", [P, DEPTH * RET_HEADS, NC, P], fp32, kind="Internal").ap()

    rows = "l (k p) c -> p l k c"
    win_v, reto_v, dilo_v, wout_v = (w.rearrange(rows, p=P) for w in (w_in, w_ret_o, w_dil_o, w_out))
    gate_v = [w.rearrange(rows, p=P) for w in (ffn1_gate, ffn2_gate)]
    up_v = [w.rearrange(rows, p=P) for w in (ffn1_up, ffn2_up)]
    down_v = [w.rearrange(rows, p=P) for w in (ffn1_down, ffn2_down)]

    ctx = ExitStack()
    with ctx:
        def sb(name, shape, dt=fp32):
            return ctx.enter_context(nc.sbuf_tensor(name, shape, dt))

        def sem(name):
            return ctx.enter_context(nc.semaphore(name))

        raw = sb("raw", [P, 2, 2048])
        w_hi = sb("w_hi", [P, 2, 2048], f32r)
        w_lo = sb("w_lo", [P, 2, 2048], f32r)
        xs = sb("xs", [P, KT, SEQ])
        h_hi = sb("h_hi", [P, KT, SEQ], f32r)
        h_lo = sb("h_lo", [P, KT, SEQ], f32r)
        y_hi = sb("y_hi", [P, 12, SEQ], f32r)
        y_lo = sb("y_lo", [P, 12, SEQ], f32r)
        mg_hi = sb("mg_hi", [P, SEQ], f32r)
        mg_lo = sb("mg_lo", [P, SEQ], f32r)
        r_b = sb("r_b", [P, SEQ])
        cos_r = sb("cos_r", [P, SEQ])
        sin_r = sb("sin_r", [P, SEQ])
        cos_t = sb("cos_t", [P, SEQ])
        sin_t = sb("sin_t", [P, SEQ])
        bias_sb = sb("bias_sb", [P, 1, NT, P])
        decay_sb = sb("decay_sb", [P, 1, NC, P])
        bias_f = bias_sb[:, :, :, :].rearrange("p o c i -> p (o c i)")
        decay_f = decay_sb[:, :, :, :].rearrange("p o c i -> p (o c i)")
        ident = sb("ident", [P, P])
        ones = sb("ones", [P, 2])
        eps_c = sb("eps_c", [P, 1])
        params = sb("params", [P, DEPTH * ROWS])
        par = sb("par", [P, ROWS])
        gq = sb("gq", [P, 1])
        work = sb("work", [P, 17, SEQ])
        flat = work[:, :, :].rearrange("p t n -> p (t n)")

        def tiny(name, n=NB):
            return sb(name, [P, n])

        n_var, n_ln, n_exp, n_a, n_b, r_col = (tiny(f"n_{k}") for k in ("var", "ln", "exp", "a", "b", "r"))
        t_var, t_ln, t_exp, t_a, t_b, t_r = (tiny(f"t_{k}") for k in ("var", "ln", "exp", "a", "b", "r"))
        NQ = 2 * DIL_GROUPS * NB
        q_raw, q_var, q_ln, q_exp, q_a, q_b, q_y, rqk, r6, rr6 = (
            tiny(f"q_{k}", NQ) for k in ("raw", "var", "ln", "exp", "a", "b", "y", "rqk", "r6", "rr6"))
        row_max, neg_max, den, rden = (tiny(k, 1) for k in ("row_max", "neg_max", "den", "rden"))
        relb = sb("relb", [N_BUCKETS + 1, 12])
        sel = sb("sel", [8, 56])
        dexp = sb("dexp", [8, 2])
        d_e, d_y, d_w, d_ln, d_d, d_s, d_s2, d_p, d_lg, d_m = (
            sb(f"d_{k}", [56, 2]) for k in ("e", "y", "w", "ln", "d", "s", "s2", "p", "lg", "m"))

        PB = [ctx.enter_context(nc.psum_tensor(f"proj{i}", [P, SEQ], fp32)) for i in range(4)]
        AB = [ctx.enter_context(nc.psum_tensor(f"acc{i}", [P, SEQ], fp32)) for i in range(4)]

        gate_s, sig, gated, hidden = (work[:, 2 * i:2 * i + 2, :] for i in range(4))
        n_sq, ssq = [work[:, 10, :], work[:, 11, :]], work[:, 12, :]
        ret_v = work[:, 0:2, :].rearrange("p t (b n) -> p (t b) n", n=RET_DV)
        silu = work[:, 2:4, :]
        dil_v = work[:, 4:7, :].rearrange("p g (b n) -> p g b n", n=P)
        s_sb = flat[:, 7 * SEQ:7 * SEQ + 768]
        p_t = flat[:, 7 * SEQ + 768:10 * SEQ]
        ret_pt = [work[:, 7, :], work[:, 8, :]]
        swap, rope_c = work[:, 10, :], work[:, 11, :]
        qk_sq = [work[:, 12, :], work[:, 13, :]]
        ret_og = [work[:, 10, :], work[:, 11, :]]
        ret_sq = [work[:, 9, :], work[:, 14, :]]
        v2_t = work[:, 15, :]
        x_tok = work[:, 0:8, :].rearrange("p t n -> p (t n)").rearrange("p (r d) -> p r d", r=NB)
        onehot = xs[0:N_BUCKETS + 1, 0:5, :].rearrange("p t n -> p (t n)")[:, 0:NT * WD]
        bdiag = work[0:12, 8:13, :].rearrange("p t n -> p (t n)")[:, 0:NT * WD]
        prow = work[0:DEPTH * ROWS, 13, 0:P]
        dist = work[0:56, 14, 0:WD]
        dpos, dneg = work[0:56, 15, 0:WD], work[0:56, 16, 0:WD]

        consts_in, x_in, ones_set = sem("consts_in"), sem("x_in"), sem("ones_set")
        relb_one = sem("relb_one")
        params_t, params_ready, dexp_t = sem("params_t"), sem("params_ready"), sem("dexp_t")
        bias_mm, bias_evicted, x_transposed = sem("bias_mm"), sem("bias_evicted"), sem("x_transposed")
        dstep, d_exp, d_log, decay_done = sem("dstep"), sem("d_exp"), sem("d_log"), sem("decay_done")
        bias_out, decay_out, bias_exp, decay_exp = (sem(k) for k in ("bias_out", "decay_out", "bias_exp", "decay_exp"))
        raw_landed = [sem("raw_landed0"), sem("raw_landed1")]
        weights_hi, weights_lo, tiles_done = sem("weights_hi"), sem("weights_lo"), sem("tiles_done")
        par_ready, h_hi_ready, h_lo_ready = sem("par_ready"), sem("h_hi_ready"), sem("h_lo_ready")
        x_squared, ssq_added, norm_sum, norm_var = (sem(k) for k in ("x_squared", "ssq_added", "norm_sum", "norm_var"))
        norm_ln, norm_exp, norm_newton, norm_bcast = (sem(k) for k in ("norm_ln", "norm_exp", "norm_newton", "norm_bcast"))
        r_ready, rope_tables, r6_ready = sem("r_ready"), sem("rope_tables"), sem("r6_ready")
        gate_scaled, sig_ready, gated_ready, up_scaled = (sem(k) for k in ("gate_scaled", "sig_ready", "gated_ready", "up_scaled"))
        hidden_ready, hid_hi, hid_lo, ffn_x = (sem(k) for k in ("hidden_ready", "hid_hi", "hid_lo", "ffn_x"))
        x_spilled, x_restored = sem("x_spilled"), sem("x_restored")
        decay_landed, bias_landed = sem("decay_landed"), sem("bias_landed")
        swapped, rope_step, ret_v_ready, rg_scaled = (sem(k) for k in ("swapped", "rope_step", "ret_v_ready", "rg_scaled"))
        rg_sig, silu_ready, ret_s, ret_p, ret_pv = (sem(k) for k in ("rg_sig", "silu_ready", "ret_s", "ret_p", "ret_pv"))
        ret_o_read, ret_sum, ret_var, ret_ln, ret_exp, ret_newton, ret_bcast = (
            sem(k) for k in ("ret_o_read", "ret_sum", "ret_var", "ret_ln", "ret_exp", "ret_newton", "ret_bcast"))
        ret_y, ret_hi, ret_lo = sem("ret_y"), sem("ret_hi"), sem("ret_lo")
        qk_squared, qk_sum, qk_var, qk_ln, qk_exp, qk_newton = (
            sem(k) for k in ("qk_squared", "qk_sum", "qk_var", "qk_ln", "qk_exp", "qk_newton"))
        k_bcast, k_scaled, v01_ready, v2_scaled, v2_turned, v2_ready = (
            sem(k) for k in ("k_bcast", "k_scaled", "v01_ready", "v2_scaled", "v2_turned", "v2_ready"))
        dil_s, dil_biased, dil_max, dil_exp, dil_recip, dil_p = (
            sem(k) for k in ("dil_s", "dil_biased", "dil_max", "dil_exp", "dil_recip", "dil_p"))
        dil_t, dil_t_act, dil_t_dve, dil_pv, dil_hi, dil_lo = (
            sem(k) for k in ("dil_t", "dil_t_act", "dil_t_dve", "dil_pv", "dil_hi", "dil_lo"))
        mg_scaled, mg_sig, mg_y, mg_sum, mg_hi_ready, mg_lo_ready, mix_x = (
            sem(k) for k in ("mg_scaled", "mg_sig", "mg_y", "mg_sum", "mg_hi_ready", "mg_lo_ready", "mix_x"))
        out_turned, out_copied, stored = sem("out_turned"), sem("out_copied"), sem("stored")

        block = ctx.enter_context(nc.Block())

        N_CONSTS = 7 + DEPTH + DEPTH * 7

        @block.sync
        def _(sp):
            def load(u, parts):
                sp.wait_ge(weights_lo, u.index + 1)
                for dst, src in parts:
                    sp.dma_start(dst, src).then_inc(raw_landed[u.slot], 16)

            def slot(u, n=2048):
                return raw[:, u.slot:u.slot + 1, 0:n]

            def cols256(u, w, layer, col):
                v = slot(u).rearrange("p o (k c) -> p o k c", c=2 * P)
                load(u, [(v[:, :, k:k + 4, :], w[:, ds(layer, 1), k:k + 4, ds(col, 2 * P)]) for k in (0, 4)])

            def two_cols128(u, w, layer, col0, col1):
                v = slot(u).rearrange("p o (k c) -> p o k c", c=2 * P)
                load(u, [(v[:, :, :, 0:P], w[:, ds(layer, 1), :, ds(col0, P)]),
                         (v[:, :, :, P:2 * P], w[:, ds(layer, 1), :, ds(col1, P)])])

            def down_rows(u, w, layer, g):
                v = slot(u).rearrange("p o (k c) -> p o k c", c=D_MODEL)
                load(u, [(v[:, :, t:t + 1, :], w[:, ds(layer, 1), ds(2 * g + t, 1), :]) for t in (0, 1)])

            def ffn(l, f):
                base = FFN_BASE[f]
                cols256(unit(l, base), gate_v[f], l, 0)
                cols256(unit(l, base + 1), up_v[f], l, 0)
                with sp.Fori(0, PAIRS) as i:
                    for j in (0, 1):
                        at = lambda k: unit(l, base + 2 + 3 * j + k, i, 6, 24)
                        down_rows(at(0), down_v[f], l, 2 * i + j)
                        cols256(at(1), gate_v[f], l, (2 * i + j + 1) * GRP)
                        cols256(at(2), up_v[f], l, (2 * i + j + 1) * GRP)
                down_rows(unit(l, base + 32), down_v[f], l, GROUPS - 1)

            def head_units(l, n):
                at = lambda k: unit(l, HEAD_BASE + k, n, 8, 19)
                two_cols128(at(0), win_v, l, C_RQ + n * P, C_RK + n * P)
                cols256(at(1), win_v, l, C_RV + n * RET_DV)
                sp.wait_ge(ret_p, 4 * (4 * l + n) + FREE)
                sp.dma_start(decay_sb[:, :, :, :], decay_full[:, ds(4 * l + n, 1), :, :]).then_inc(decay_landed, 16)
                cols256(at(2), win_v, l, C_RG + n * RET_DV)
                for g in range(DIL_GROUPS):
                    col = 4 * g * P + n * P
                    two_cols128(at(3 + g), win_v, l, C_DQ + col, C_DK + col)
                v = slot(at(6), 1024).rearrange("p o (k c) -> p o k c", c=P)
                load(at(6), [(v[:, :, k:k + 4, :], win_v[:, ds(l, 1), k:k + 4, ds(C_DV + 8 * P + n * P, P)]) for k in (0, 4)])
                two_cols128(at(7), win_v, l, C_DV + n * P, C_DV + 4 * P + n * P)
                sp.wait_ge(dil_biased, 12 * (4 * l + n) + FREE)
                sp.dma_start(bias_sb[:, :, :, :], bias_full[:, ds(n, 1), :, :]).then_inc(bias_landed, 16)

            def merge_gates(u, l, m):
                two_cols128(u, win_v, l, C_GR + m * P, C_GD + m * P)

            def merge_outs(u, l, m):
                v = slot(u, 1536).rearrange("p o (k c) -> p o k c", c=P)
                load(u, [(v[:, :, 0:8, :], reto_v[:, ds(l, 1), :, ds(m * P, P)]),
                         (v[:, :, 8:12, :], dilo_v[:, ds(l, 1), :, ds(m * P, P)])])

            def merge_wout(u, l, m):
                v = slot(u, 1024).rearrange("p o (k c) -> p o k c", k=1)
                load(u, [(v[:, :, :, c:c + 512], wout_v[:, ds(l, 1), ds(m, 1), c:c + 512]) for c in (0, 512)])

            with sp.Fori(0, DEPTH) as l:
                ffn(l, 0)
                sp.wait_ge(decay_exp, 16 * DEPTH * RET_HEADS)
                sp.wait_ge(bias_exp, 16 * 2 * DIL_HPG)
                with sp.Fori(0, RET_HEADS) as n:
                    head_units(l, n)
                merge_gates(unit(l, MERGE_BASE), l, 0)
                merge_outs(unit(l, MERGE_BASE + 1), l, 0)
                sp.wait_ge(x_spilled, 16 * (l + 1))
                sp.wait_ge(dil_s, 16 * (l + 1))
                sp.dma_start(xs[:, :, :], x_spill).then_inc(x_restored, 16)
                with sp.Fori(0, 3) as i:
                    for j in (0, 1):
                        at = lambda k: unit(l, MERGE_BASE + 2 + 3 * j + k, i, 6, 24)
                        merge_wout(at(0), l, 2 * i + j)
                        merge_gates(at(1), l, 2 * i + j + 1)
                        merge_outs(at(2), l, 2 * i + j + 1)
                merge_wout(unit(l, MERGE_BASE + 20), l, 6)
                merge_gates(unit(l, MERGE_BASE + 21), l, 7)
                merge_outs(unit(l, MERGE_BASE + 22), l, 7)
                merge_wout(unit(l, MERGE_BASE + 23), l, 7)
                ffn(l, 1)
            sp.wait_ge(out_copied, 8)
            sp.dma_start(out.rearrange("(i r) d -> i r d", r=NB), x_tok).then_inc(stored, 16)
            sp.wait_ge(stored, 16)

        @block.gpsimd
        def _(pool):
            pool.wait_ge(bias_evicted, 5)
            pool.dma_start(bias_diag.ap(), bdiag).then_inc(bias_out, 16)
            pool.wait_ge(bias_out, 16)
            for j in range(DIL_HPG):
                first = bass.AP(bias_diag, j * NT * WD + P - 1, [[WD, NC], [-1, P], [1, P]])
                pool.dma_start(bias_full[:, j, 0:NC, :].rearrange("p c i -> c p i"), first).then_inc(bias_exp, 16)
                rest = bass.AP(bias_diag, (DIL_HPG + j) * NT * WD + NC * WD + P - 1,
                               [[DIL_HPG * NT * WD + WD, 2], [-1, P], [1, P]])
                pool.dma_start(bias_full[:, j, NC:NT, :].rearrange("p c i -> c p i"), rest).then_inc(bias_exp, 16)
            pool.wait_ge(decay_done, 1)
            pool.dma_start(decay_diag.ap(), dpos).then_inc(decay_out, 16)
            pool.wait_ge(decay_out, 16)
            for j in range(DEPTH * RET_HEADS):
                src = bass.AP(decay_diag, j * NC * WD + P - 1, [[WD, NC], [-1, P], [1, P]])
                pool.dma_start(decay_full[:, j, :, :].rearrange("p c i -> c p i"), src).then_inc(decay_exp, 16)
            pool.wait_ge(bias_exp, 16 * 2 * DIL_HPG)
            pool.wait_ge(decay_exp, 16 * DEPTH * RET_HEADS)

        @block.tensor
        def _(pe):
            def three(o, s_hi, s_lo, m_hi, m_lo, start, stop):
                pe.matmul(o, s_hi, m_hi, start=start, stop=False)
                pe.matmul(o, s_hi, m_lo, start=False, stop=False)
                return pe.matmul(o, s_lo, m_hi, start=False, stop=stop)

            def begin(u):
                pe.wait_ge(weights_lo, u.index + 1 + LO_CREDIT)

            def tile_cols(u, bank, t, fresh=None, width=2 * P):
                for k in range(KT):
                    if fresh is not None:
                        pe.wait_ge(h_lo_ready, 8 * fresh + k + 1 + FREE)
                    c = k * width + t * P
                    last = three(bank[:, :], w_hi[:, u.slot, c:c + P], w_lo[:, u.slot, c:c + P],
                                 h_hi[:, k, :], h_lo[:, k, :], k == 0, k == KT - 1)
                last.then_inc(tiles_done, 1)

            def tile_tokens(u, bank, b):
                for k in range(KT):
                    c, t = k * 2 * P, slice(b * P, (b + 1) * P)
                    last = three(bank[:, 0:2 * P], h_hi[:, k, t], h_lo[:, k, t],
                                 w_hi[:, u.slot, c:c + 2 * P], w_lo[:, u.slot, c:c + 2 * P], k == 0, k == KT - 1)
                last.then_inc(tiles_done, 1)

            def norm_sums(N):
                pe.wait_ge(ssq_added, 8 * N + 8)
                for b in range(NB):
                    last = pe.matmul(AB[0][:, b:b + 1], ssq[:, b * P:(b + 1) * P], ones[:, 0:1], start=True, stop=True)
                last.then_inc(norm_sum, 1)

            def spread(bank, col):
                for b in range(NB):
                    last = pe.matmul(bank[:, b * P:(b + 1) * P], col(b).to_broadcast([P, P]), ident[:, :],
                                     start=True, stop=True)
                return last

            def norm_spread(N):
                pe.wait_ge(norm_newton, 3 * N + 3)
                spread(AB[1], lambda b: r_col[:, b:b + 1]).then_inc(norm_bcast, 1)

            def ffn(l, f):
                base, q0, N = FFN_BASE[f], (2 * l + f) * GROUPS, 3 * l + 2 * f

                def gate(u, q, first=False):
                    begin(u)
                    for t in (0, 1):
                        pe.wait_ge(gate_scaled, 2 * q + t + 1)
                        tile_cols(u, PB[t], t, N if first else None)

                def up(u, q, t):
                    pe.wait_ge(up_scaled, 2 * q + t + 1)
                    tile_cols(u, PB[2 + t], t)

                def down(u, q):
                    begin(u)
                    for m in range(KT):
                        pe.wait_ge(ffn_x, 8 * q + m + 5)
                        for t in (0, 1):
                            if m == 0:
                                pe.wait_ge(hid_lo, 2 * q + t + 1)
                            c = t * D_MODEL + m * P
                            last = three(AB[m % 4][:, :], w_hi[:, u.slot, c:c + P], w_lo[:, u.slot, c:c + P],
                                         y_hi[:, t, :], y_lo[:, t, :], t == 0, t == 1)
                        last.then_inc(tiles_done, 1)

                gate(unit(l, base), q0, True)
                norm_sums(N)
                begin(unit(l, base + 1))
                up(unit(l, base + 1), q0, 0)
                norm_spread(N)
                up(unit(l, base + 1), q0, 1)
                with pe.Fori(0, PAIRS) as i:
                    for j in (0, 1):
                        at = lambda k: unit(l, base + 2 + 3 * j + k, i, 6, 24)
                        q = q0 + 2 * i + j
                        down(at(0), q)
                        gate(at(1), q + 1)
                        begin(at(2))
                        up(at(2), q + 1, 0)
                        up(at(2), q + 1, 1)
                down(unit(l, base + 32), q0 + GROUPS - 1)

            def dil_scores(H, b):
                if b == 0:
                    pe.wait_ge(k_scaled, 3 * H + 3)
                else:
                    pe.wait_ge(dil_biased, 12 * H + 3 * b + FREE)
                    pe.wait_ge(dil_t_dve, 4 * H + b + FREE)
                t = slice(b * P, (b + 1) * P)
                pe.matmul(AB[0][:, :], xs[:, 0, t], xs[:, 1, :], start=True, stop=True)
                pe.matmul(AB[1][:, 0:P], xs[:, 2, t], xs[:, 3, t], start=True, stop=True)
                pe.matmul(AB[1][:, P:2 * P], xs[:, 4, t], xs[:, 5, t], start=True, stop=True).then_inc(dil_s, 1)

            def dil_turn(H, b):
                pe.wait_ge(dil_p, 4 * H + b + 1)
                if b:
                    pe.wait_ge(dil_t_act, 4 * H + b)
                for c in range(4):
                    pe.transpose(AB[2][:, c * P:(c + 1) * P], s_sb[:, c * P:(c + 1) * P], ident[:, :])
                for c in (4, 5):
                    last = pe.transpose(AB[1][:, (c - 2) * P:(c - 1) * P], s_sb[:, c * P:(c + 1) * P], ident[:, :])
                last.then_inc(dil_t, 1)

            def dil_values(H, b):
                if b == 0:
                    pe.wait_ge(v01_ready, 4 * H + 4 + 4)
                    pe.wait_ge(v2_ready, H + 1)
                    pe.wait_ge(ret_y, 4 * H + 2)
                pe.wait_ge(dil_t_act, 4 * H + b + 1)
                pe.wait_ge(dil_t_dve, 4 * H + b + 1 + FREE)
                o = AB[3][:, b * P:(b + 1) * P]
                for a in range(NB):
                    pe.matmul(o, dil_v[:, 0, a, :], p_t[:, a * P:(a + 1) * P], start=a == 0, stop=False)
                pe.matmul(o, dil_v[:, 1, b, :], p_t[:, 4 * P:5 * P], start=False, stop=False)
                pe.matmul(o, dil_v[:, 2, b, :], p_t[:, 5 * P:6 * P], start=False, stop=True).then_inc(dil_pv, 1)

            def ret_scores(H, a):
                if a == 0:
                    pe.wait_ge(rope_step, 6 * H + 6)
                    pe.wait_ge(dil_biased, 12 * H + FREE)
                else:
                    pe.wait_ge(ret_p, 4 * H + a + FREE)
                pe.matmul(AB[0][:, :], xs[:, 7, a * P:(a + 1) * P], xs[:, 6, :], start=True, stop=True).then_inc(ret_s, 1)

            def ret_values(H, a):
                if a == 0:
                    pe.wait_ge(ret_v_ready, 4 * H + 4)
                    pe.wait_ge(dil_lo, H + FREE)
                pe.wait_ge(ret_p, 4 * H + a + 1 + FREE)
                for e in (0, 1):
                    last = pe.matmul(AB[2 + e][:, :], ret_v[:, a, e * P:(e + 1) * P], ret_pt[a % 2], start=a == 0,
                                     stop=a == NB - 1)
                last.then_inc(ret_pv, 1)

            def qk_sums(H, i):
                if i == 0:
                    pe.wait_ge(dil_t_dve, 4 * H + FREE)
                pe.wait_ge(qk_squared, 6 * H + i + 1)
                for b in range(NB):
                    last = pe.matmul(AB[1][:, 4 * i + b:4 * i + b + 1], qk_sq[i % 2][:, b * P:(b + 1) * P], ones[:, 0:1],
                                     start=True, stop=True)
                last.then_inc(qk_sum, 1)

            def k_spread(H, g, bank):
                spread(bank, lambda b: rqk[:, (2 * g + 1) * NB + b:(2 * g + 1) * NB + b + 1]).then_inc(k_bcast, 1)

            def heads(l, n, prev, first=None):
                H = 4 * l + n
                at = lambda k: unit(l, HEAD_BASE + k, n, 8, 19)
                u = at(0)
                begin(u)
                pe.wait_ge(v01_ready, 4 * H + 2)
                tile_cols(u, PB[0], 0, first)
                if prev:
                    dil_scores(H - 1, 0)
                pe.wait_ge(v01_ready, 4 * H + 3)
                tile_cols(u, PB[1], 1)
                if prev:
                    dil_turn(H - 1, 0)
                if first is not None:
                    norm_sums(first)
                u = at(1)
                begin(u)
                pe.wait_ge(v01_ready, 4 * H + 4)
                tile_tokens(u, PB[2], 0)
                if prev:
                    dil_values(H - 1, 0)
                    dil_scores(H - 1, 1)
                tile_tokens(u, PB[3], 1)
                if first is not None:
                    norm_spread(first)
                pe.wait_ge(rope_step, 6 * H + 1)
                tile_tokens(u, PB[0], 2)
                if prev:
                    dil_turn(H - 1, 1)
                pe.wait_ge(rope_step, 6 * H + 4)
                tile_tokens(u, PB[1], 3)
                if prev:
                    dil_values(H - 1, 1)
                    dil_scores(H - 1, 2)
                u = at(2)
                begin(u)
                pe.wait_ge(ret_v_ready, 4 * H + 1)
                tile_cols(u, PB[2], 0)
                if prev:
                    dil_turn(H - 1, 2)
                pe.wait_ge(ret_v_ready, 4 * H + 2)
                tile_cols(u, PB[3], 1)
                if prev:
                    dil_values(H - 1, 2)
                    dil_scores(H - 1, 3)
                u = at(3)
                begin(u)
                pe.wait_ge(ret_v_ready, 4 * H + 3)
                tile_cols(u, PB[0], 0)
                if prev:
                    dil_turn(H - 1, 3)
                pe.wait_ge(ret_v_ready, 4 * H + 4)
                tile_cols(u, PB[1], 1)
                if prev:
                    dil_values(H - 1, 3)
                ret_scores(H, 0)
                u = at(4)
                begin(u)
                pe.wait_ge(rg_scaled, 2 * H + 1)
                tile_cols(u, PB[2], 0)
                qk_sums(H, 0)
                ret_scores(H, 1)
                ret_values(H, 0)
                pe.wait_ge(rg_scaled, 2 * H + 2)
                tile_cols(u, PB[3], 1)
                qk_sums(H, 1)
                ret_scores(H, 2)
                ret_values(H, 1)
                u = at(5)
                begin(u)
                pe.wait_ge(qk_squared, 6 * H + 1)
                tile_cols(u, PB[0], 0)
                qk_sums(H, 2)
                ret_scores(H, 3)
                ret_values(H, 2)
                pe.wait_ge(qk_squared, 6 * H + 2)
                tile_cols(u, PB[1], 1)
                qk_sums(H, 3)
                ret_values(H, 3)
                u = at(6)
                begin(u)
                pe.wait_ge(qk_squared, 6 * H + 3)
                tile_cols(u, PB[2], 0, width=P)
                qk_sums(H, 4)
                u = at(7)
                begin(u)
                pe.wait_ge(qk_squared, 6 * H + 4)
                tile_tokens(u, PB[3], 0)
                qk_sums(H, 5)
                pe.wait_ge(ret_o_read, 4 * H + 4)
                pe.wait_ge(ret_p, 4 * H + 4 + FREE)
                for b in range(NB):
                    for e in (0, 1):
                        last = pe.matmul(AB[0][:, b:b + 1], ret_sq[e][:, b * P:(b + 1) * P], ones[:, 0:1],
                                         start=e == 0, stop=e == 1)
                last.then_inc(ret_sum, 1)
                pe.wait_ge(qk_squared, 6 * H + 5)
                tile_tokens(u, PB[0], 1)
                pe.wait_ge(v2_scaled, H + 1)
                for b in range(NB):
                    last = pe.transpose(AB[2][:, b * P:(b + 1) * P], v2_t[:, b * P:(b + 1) * P], ident[:, :])
                last.then_inc(v2_turned, 1)
                pe.wait_ge(qk_squared, 6 * H + 6)
                tile_tokens(u, PB[1], 2)
                pe.wait_ge(ret_newton, 3 * H + 3)
                spread(AB[3], lambda b: t_r[:, b:b + 1]).then_inc(ret_bcast, 1)
                pe.wait_ge(qk_newton, 4 * H + 4)
                k_spread(H, 0, AB[1])
                tile_tokens(u, PB[2], 3)
                k_spread(H, 1, AB[0])
                pe.wait_ge(v2_ready, H + 1)
                k_spread(H, 2, AB[2])

            def last_attention(H):
                for b in range(NB):
                    dil_scores(H, b)
                    dil_turn(H, b)
                    dil_values(H, b)

            def merge(l):
                def branches(ug, uo, M, start=False):
                    begin(ug)
                    for t in (0, 1):
                        pe.wait_ge(mg_scaled, 2 * M + t + 1)
                        tile_cols(ug, PB[t], t)
                    begin(uo)
                    if start:
                        pe.wait_ge(ret_lo, 8 * (l + 1) + FREE)
                    pe.wait_ge(mg_y, 2 * M + 1)
                    for k in range(8):
                        last = three(PB[2][:, :], w_hi[:, uo.slot, k * P:(k + 1) * P], w_lo[:, uo.slot, k * P:(k + 1) * P],
                                     y_hi[:, k, :], y_lo[:, k, :], k == 0, k == 7)
                    last.then_inc(tiles_done, 1)
                    if start:
                        pe.wait_ge(dil_lo, 4 * (l + 1) + FREE)
                    pe.wait_ge(mg_y, 2 * M + 2)
                    for k in range(8, 12):
                        last = three(PB[3][:, :], w_hi[:, uo.slot, k * P:(k + 1) * P], w_lo[:, uo.slot, k * P:(k + 1) * P],
                                     y_hi[:, k, :], y_lo[:, k, :], k == 8, k == 11)
                    last.then_inc(tiles_done, 1)

                def wout(u, M):
                    begin(u)
                    pe.wait_ge(mg_lo_ready, M + 1)
                    for m in range(KT):
                        pe.wait_ge(mix_x, 8 * M + m + 5)
                        c = m * P
                        three(AB[m % 4][:, :], w_hi[:, u.slot, c:c + P], w_lo[:, u.slot, c:c + P],
                              mg_hi[:, :], mg_lo[:, :], True, True).then_inc(tiles_done, 1)

                M0 = KT * l
                pe.wait_ge(v01_ready, 4 * 4 * (l + 1) + 4)
                branches(unit(l, MERGE_BASE), unit(l, MERGE_BASE + 1), M0, True)
                with pe.Fori(0, 3) as i:
                    for j in (0, 1):
                        at = lambda k: unit(l, MERGE_BASE + 2 + 3 * j + k, i, 6, 24)
                        M = M0 + 2 * i + j
                        wout(at(0), M)
                        branches(at(1), at(2), M + 1)
                wout(unit(l, MERGE_BASE + 20), M0 + 6)
                branches(unit(l, MERGE_BASE + 21), unit(l, MERGE_BASE + 22), M0 + 7)
                wout(unit(l, MERGE_BASE + 23), M0 + 7)

            pe.sem_inc(tiles_done, FIRST_CREDIT)
            pe.sem_inc(dil_pv, FREE)
            pe.wait_ge(consts_in, 16 * N_CONSTS)
            pe.wait_ge(relb_one, 1)
            pe.matmul(AB[1][0:56, 0:2], sel[:, :], dexp[:, :], start=True, stop=True).then_inc(dexp_t, 1)
            pe.transpose(AB[0][:, 0:DEPTH * ROWS], prow, ident[0:DEPTH * ROWS, 0:DEPTH * ROWS]).then_inc(params_t, 1)
            for c, bank in enumerate((PB[0], PB[1], PB[2], PB[3], AB[2])):
                w = min(512, NT * WD - 512 * c)
                pe.matmul(bank[0:12, 0:w], relb[:, :], onehot[:, 512 * c:512 * c + w], start=True, stop=True).then_inc(bias_mm, 1)
            pe.wait_ge(x_in, 16)
            for m in range(KT):
                if m < 4:
                    pe.wait_ge(bias_evicted, m + 1)
                else:
                    pe.wait_ge(ffn_x, m - 3)
                for r in range(NB):
                    last = pe.transpose(PB[m % 4][:, r * P:(r + 1) * P], x_tok[:, r, m * P:(m + 1) * P], ident[:, :])
                last.then_inc(x_transposed, 1)
            pe.wait_ge(ones_set, 1)
            pe.wait_ge(ffn_x, 8)
            with pe.Fori(0, DEPTH) as l:
                ffn(l, 0)
                heads(l, 0, False, 3 * l + 1)
                with pe.Fori(1, RET_HEADS) as n:
                    heads(l, n, True)
                last_attention(4 * l + 3)
                merge(l)
                ffn(l, 1)
            pe.wait_ge(ffn_x, 8 + 8 * GROUPS * 2 * DEPTH)
            for r in range(NB):
                for half in (0, 1):
                    n = 2 * r + half
                    if n >= 4:
                        pe.wait_ge(out_copied, n - 3)
                    for m in range(4):
                        last = pe.transpose(AB[n % 4][:, m * P:(m + 1) * P], xs[:, 4 * half + m, r * P:(r + 1) * P], ident[:, :])
                    last.then_inc(out_turned, 1)

        @block.scalar
        def _(act):
            def split(u, n=2048):
                act.wait_ge(raw_landed[u.slot], 32 * (u.turn + 1))
                act.wait_ge(tiles_done, u.tile - u.before + FIRST_CREDIT)
                act.activation(w_hi[:, u.slot, 0:n], raw[:, u.slot, 0:n], ACT.Copy).then_inc(weights_hi, 1)

            def done(tile):
                act.wait_ge(tiles_done, tile + 1 + FIRST_CREDIT)

            def start_norm(N, k, x_ready):
                for m in range(KT):
                    act.wait_ge(*x_ready(m))
                    act.activation(h_hi[:, m, :], xs[:, m, :], ACT.Copy,
                                   scale=par[:, R_N[k] + m:R_N[k] + m + 1]).then_inc(h_hi_ready, 1)
                for m in range(KT):
                    if m >= 2:
                        act.wait_ge(ssq_added, 8 * N + m - 1)
                    act.activation(n_sq[m % 2], xs[:, m, :], ACT.Square).then_inc(x_squared, 1)

            def norm_factor(N):
                act.wait_ge(norm_var, N + 1)
                act.activation(n_ln[:, :], n_var[:, :], ACT.Ln).then_inc(norm_ln, 1)
                act.wait_ge(norm_ln, N + 1)
                act.activation(n_exp[:, :], n_ln[:, :], ACT.Exp, scale=-0.5).then_inc(norm_exp, 1)

            def norm_copy(N):
                act.wait_ge(norm_bcast, N + 1)
                act.activation(r_b[:, :], AB[1][:, :], ACT.Copy).then_inc(r_ready, 1)

            def ffn(l, f):
                base, q0, N = FFN_BASE[f], (2 * l + f) * GROUPS, 3 * l + 2 * f

                def sigmoids(q):
                    for t in (0, 1):
                        act.wait_ge(gate_scaled, 2 * q + t + 1 + 2)
                        act.activation(sig[:, t, :], gate_s[:, t, :], ACT.Sigmoid).then_inc(sig_ready, 1)

                def hidden_his(q):
                    for t in (0, 1):
                        act.wait_ge(hidden_ready, 2 * q + t + 1)
                        act.activation(y_hi[:, t, :], hidden[:, t, :], ACT.Copy).then_inc(hid_hi, 1)

                split(unit(l, base + 1))
                norm_factor(N)
                norm_copy(N)
                sigmoids(q0)
                split(unit(l, base + 2))
                hidden_his(q0)
                with act.Fori(0, PAIRS) as i:
                    for j in (0, 1):
                        at = lambda k: unit(l, base + 2 + 3 * j + k, i, 6, 24)
                        q = q0 + 2 * i + j
                        split(at(1))
                        split(at(2))
                        sigmoids(q + 1)
                        split(unit(l, base + 2 + 3 * j + 3, i, 6, 24))
                        hidden_his(q + 1)
                if f == 0:
                    split(unit(l, base + 33))

            def dil_exps(H, b):
                act.wait_ge(dil_max, 8 * H + 2 * b + 2)
                act.activation(s_sb, s_sb, ACT.Exp, bias=neg_max[:, 0:1], accum_out=den[:, 0:1]).then_inc(dil_exp, 1)

            def dil_copy(H, b):
                act.wait_ge(dil_t, 4 * H + b + 1)
                act.wait_ge(dil_pv, 4 * H + b + FREE)
                act.activation(p_t[:, 0:512], AB[2][:, :], ACT.Copy).then_inc(dil_t_act, 1)

            def dil_out(H, j):
                act.wait_ge(dil_pv, 4 * H + 4 + FREE)
                act.activation(y_hi[:, ds(8 + j, 1), :], AB[3][:, :].unsqueeze(1), ACT.Copy).then_inc(dil_hi, 1)

            def swap_halves(H, i, tile):
                done(tile)
                if i == 0:
                    act.wait_ge(ret_lo, 2 * H + FREE)
                else:
                    act.wait_ge(rope_step, 6 * H + 3)
                act.activation(swap[0:64, :], PB[i][64:128, :], ACT.Copy).then_inc(swapped, 1)
                act.activation(swap[64:128, :], PB[i][0:64, :], ACT.Copy).then_inc(swapped, 1)

            def ret_values(H, b, tile, bank):
                done(tile)
                act.activation(ret_v[:, b, :], bank[:, 0:RET_DV], ACT.Copy, scale=r_col[:, b:b + 1]).then_inc(ret_v_ready, 1)

            def qk_tile(H, i, tile, bank):
                done(tile)
                act.activation(xs[:, i, :], bank[:, :], ACT.Copy,
                               scale=gq[:, 0:1] if i % 2 == 0 else par[:, R_KN:R_KN + 1])
                if i >= 2:
                    act.wait_ge(qk_sum, 6 * H + i - 1)
                act.activation(qk_sq[i % 2], bank[:, :], ACT.Square).then_inc(qk_squared, 1)

            def v01(H, b, tile, bank):
                done(tile)
                act.activation(dil_v[:, 0:2, b, :], bank[:, 0:2 * P].rearrange("p (g n) -> p g n", g=2), ACT.Copy,
                               scale=r_col[:, b:b + 1]).then_inc(v01_ready, 1)

            def heads(l, n, prev, first=None):
                H = 4 * l + n
                at = lambda k: unit(l, HEAD_BASE + k, n, 8, 19)
                T = at(0).tile
                split(at(1))
                if first is not None:
                    norm_factor(first)
                    norm_copy(first)
                swap_halves(H, 0, T)
                if prev:
                    dil_exps(H - 1, 0)
                swap_halves(H, 1, T + 1)
                if prev:
                    dil_copy(H - 1, 0)
                split(at(2))
                ret_values(H, 0, T + 2, PB[2])
                if prev:
                    dil_exps(H - 1, 1)
                ret_values(H, 1, T + 3, PB[3])
                ret_values(H, 2, T + 4, PB[0])
                if prev:
                    dil_copy(H - 1, 1)
                ret_values(H, 3, T + 5, PB[1])
                if prev:
                    dil_exps(H - 1, 2)
                split(at(3))
                if prev:
                    dil_copy(H - 1, 2)
                    dil_exps(H - 1, 3)
                for e in (0, 1):
                    act.wait_ge(rope_step, 6 * H + 6)
                    act.wait_ge(rg_scaled, 2 * H + e + 1)
                    act.activation(work[:, 10 + e, :], silu[:, e, :], ACT.Sigmoid).then_inc(rg_sig, 1)
                if prev:
                    dil_copy(H - 1, 3)
                split(at(4))
                act.wait_ge(x_spilled, 16 * (l + 1))
                qk_tile(H, 0, T + 8, PB[0])
                if prev:
                    dil_out(H - 1, n - 1)
                qk_tile(H, 1, T + 9, PB[1])
                split(at(5))
                qk_tile(H, 2, T + 10, PB[2])
                qk_tile(H, 3, T + 11, PB[3])
                split(at(6), 1024)
                qk_tile(H, 4, T + 12, PB[0])
                qk_tile(H, 5, T + 13, PB[1])
                act.wait_ge(ret_pv, 4 * H + 4)
                for e in (0, 1):
                    act.activation(ret_sq[e], AB[2 + e][:, :], ACT.Square).then_inc(ret_o_read, 1)
                for e in (0, 1):
                    act.activation(ret_og[e], AB[2 + e][:, :], ACT.Copy,
                                   scale=par[:, ds(2 * n + R_RN + e, 1)]).then_inc(ret_o_read, 1)
                split(at(7))
                v01(H, 0, T + 15, PB[3])
                act.wait_ge(ret_var, H + 1)
                act.activation(t_ln[:, :], t_var[:, :], ACT.Ln).then_inc(ret_ln, 1)
                act.wait_ge(ret_ln, H + 1)
                act.activation(t_exp[:, :], t_ln[:, :], ACT.Exp, scale=-0.5).then_inc(ret_exp, 1)
                act.wait_ge(qk_var, 2 * H + 2)
                act.activation(q_ln[:, :], q_var[:, :], ACT.Ln).then_inc(qk_ln, 1)
                act.wait_ge(qk_ln, H + 1)
                act.activation(q_exp[:, :], q_ln[:, :], ACT.Exp, scale=-0.5).then_inc(qk_exp, 1)
                v01(H, 1, T + 16, PB[0])
                act.wait_ge(v2_turned, H + 1)
                act.activation(dil_v[:, 2, :, :].rearrange("p b n -> p (b n)"), AB[2][:, :], ACT.Copy).then_inc(v2_ready, 1)
                split(at(8))
                v01(H, 2, T + 17, PB[1])
                v01(H, 3, T + 18, PB[2])
                for e in (0, 1):
                    act.wait_ge(ret_y, 4 * H + 3 + e)
                    act.activation(y_hi[:, ds(2 * n + e, 1), :], ret_og[e].unsqueeze(1), ACT.Copy).then_inc(ret_hi, 1)

            def merge(l):
                def gates(M, m):
                    for t in (0, 1):
                        act.wait_ge(mg_scaled, 2 * M + t + 1 + 2)
                        act.activation(sig[:, t, :], gate_s[:, t, :], ACT.Sigmoid,
                                       bias=par[:, ds(m + R_BG + KT * t, 1)]).then_inc(mg_sig, 1)

                def merged_hi(M):
                    act.wait_ge(mg_sum, M + 1)
                    act.activation(mg_hi[:, :], work[:, 6, :], ACT.Copy).then_inc(mg_hi_ready, 1)

                M0 = KT * l
                split(unit(l, MERGE_BASE + 1), 1536)
                gates(M0, 0)
                split(unit(l, MERGE_BASE + 2), 1024)
                merged_hi(M0)
                with act.Fori(0, 3) as i:
                    for j in (0, 1):
                        at = lambda k: unit(l, MERGE_BASE + 2 + 3 * j + k, i, 6, 24)
                        split(at(1))
                        split(at(2), 1536)
                        gates(M0 + 2 * i + j + 1, 2 * i + j + 1)
                        split(unit(l, MERGE_BASE + 5 + 3 * j, i, 6, 24), 1024)
                        merged_hi(M0 + 2 * i + j + 1)
                split(unit(l, MERGE_BASE + 21))
                split(unit(l, MERGE_BASE + 22), 1536)
                gates(M0 + 7, 7)
                split(unit(l, MERGE_BASE + 23), 1024)
                merged_hi(M0 + 7)
                split(unit(l, MERGE_BASE + 24))

            act.sem_inc(v01_ready, 4)
            row = 0
            for dst, src in ((ident[:, :], c_ident), (cos_t[:, :], c_cos), (sin_t[:, :], c_sin), (onehot, c_onehot),
                             (dist, c_dist), (sel[:, :], c_sel), (relb[0:N_BUCKETS, :], rel_bias)):
                act.dma_start(dst, src).then_inc(consts_in, 16)
            for l in range(DEPTH):
                act.dma_start(dexp[4 * l:4 * l + 4, :], ret_decay_exp[l].rearrange("d h -> h d"),
                              allow_slow_non_contiguous=True).then_inc(consts_in, 16)
                for w in (norm_ffn1, norm_mix, norm_ffn2, b_gate, ret_norm, dil_q_norm, dil_k_norm):
                    n = w.shape[1] // P
                    act.dma_start(prow[row:row + n, :], w[l].rearrange("(m p) -> m p", p=P)).then_inc(consts_in, 16)
                    row += n
            act.dma_start(x_tok, x[0].rearrange("(i r) d -> i r d", r=NB)).then_inc(x_in, 16)
            act.wait_ge(dstep, 1)
            act.activation(d_y[:, :], d_e[:, :], ACT.Exp, scale=-math.log(2.0)).then_inc(d_exp, 1)
            act.wait_ge(dstep, 2)
            act.activation(d_ln[:, :], d_w[:, :], ACT.Ln).then_inc(d_log, 1)
            act.wait_ge(d_log, 2)
            act.activation(dpos, dpos, ACT.Exp).then_inc(decay_done, 1)
            act.wait_ge(params_ready, 1)
            act.wait_ge(bias_out, 16)
            act.wait_ge(decay_out, 16)
            with act.Fori(0, DEPTH) as l:
                act.wait_ge(h_lo_ready, 24 * l + FREE)
                act.activation(par[:, :], params[:, ds(ROWS * l, ROWS)], ACT.Copy).then_inc(par_ready, 1)
                act.wait_ge(par_ready, 2 * l + 1)
                act.activation(gq[:, :], par[:, R_QN:R_QN + 1], ACT.Copy, scale=DIL_DH ** -0.5).then_inc(par_ready, 1)
                split(unit(l, 0))
                start_norm(3 * l, 0, lambda m: (ffn_x, 8 * GROUPS * 2 * l + m + 1))
                ffn(l, 0)
                start_norm(3 * l + 1, 1, lambda m: (ffn_x, 8 * GROUPS * (2 * l + 1) + m + 1))
                act.dma_start(x_spill, xs[:, :, :]).then_inc(x_spilled, 16)
                heads(l, 0, False, 3 * l + 1)
                with act.Fori(1, RET_HEADS) as n:
                    heads(l, n, True)
                for b in range(NB):
                    dil_exps(4 * l + 3, b)
                    dil_copy(4 * l + 3, b)
                dil_out(4 * l + 3, 3)
                merge(l)
                start_norm(3 * l + 2, 2, lambda m: (mix_x, 8 * KT * (l + 1) - KT + m + 1 + 8))
                ffn(l, 1)

        @block.vector
        def _(dve):
            def split(u, n=2048):
                dve.wait_ge(weights_hi, u.index + 1)
                dve.tensor_tensor(w_lo[:, u.slot, 0:n], raw[:, u.slot, 0:n], w_hi[:, u.slot, 0:n].bitcast(fp32),
                                  ALU.subtract).then_inc(weights_lo, 1)

            def done(tile):
                dve.wait_ge(tiles_done, tile + 1 + FIRST_CREDIT)

            def gained_lo(N, k, m):
                dve.wait_ge(h_hi_ready, 8 * N + m + 1)
                dve.scalar_tensor_tensor(h_lo[:, m, :], xs[:, m, :], par[:, R_N[k] + m:R_N[k] + m + 1],
                                         h_hi[:, m, :].bitcast(fp32), ALU.mult, ALU.subtract).then_inc(h_lo_ready, 1)

            def add_squares(N):
                for m in range(KT):
                    dve.wait_ge(x_squared, 8 * N + m + 1)
                    if m == 0:
                        dve.tensor_copy(ssq, n_sq[0]).then_inc(ssq_added, 1)
                    else:
                        dve.wait_ge(ssq_added, 8 * N + m)
                        dve.tensor_tensor(ssq, ssq, n_sq[m % 2], ALU.add).then_inc(ssq_added, 1)

            def newton(y, y0, a, b, var, counter, at):
                dve.scalar_tensor_tensor(a[:, :], y0[:, :], -0.5, y0[:, :], ALU.mult, ALU.mult).then_inc(counter, 1)
                dve.wait_ge(counter, at + 1)
                dve.tensor_tensor(b[:, :], a[:, :], var[:, :], ALU.mult).then_inc(counter, 1)
                dve.wait_ge(counter, at + 2)
                dve.scalar_tensor_tensor(y[:, :], b[:, :], 1.5, y0[:, :], ALU.add, ALU.mult).then_inc(counter, 1)

            def norm_factor(N):
                dve.wait_ge(norm_sum, N + 1)
                dve.tensor_scalar(n_var[:, :], AB[0][:, 0:NB], 1.0 / D_MODEL, EPS, ALU.mult, ALU.add).then_inc(norm_var, 1)
                dve.wait_ge(norm_exp, N + 1)
                newton(r_col, n_exp, n_a, n_b, n_var, norm_newton, 3 * N)

            def ffn(l, f, norm_after):
                base, q0, N = FFN_BASE[f], (2 * l + f) * GROUPS, 3 * l + 2 * f

                def gates(u, q):
                    for t in (0, 1):
                        done(u.tile + t)
                        dve.tensor_tensor(gate_s[:, t, :], PB[t][:, :], r_b[:, :], ALU.mult).then_inc(gate_scaled, 1)
                    for t in (0, 1):
                        dve.wait_ge(sig_ready, 2 * q + t + 1)
                        dve.tensor_tensor(gated[:, t, :], gate_s[:, t, :], sig[:, t, :], ALU.mult).then_inc(gated_ready, 1)

                def ups(u, q):
                    for t in (0, 1):
                        done(u.tile + t)
                        dve.tensor_tensor(hidden[:, t, :], PB[2 + t][:, :], r_b[:, :], ALU.mult).then_inc(up_scaled, 1)
                        dve.wait_ge(up_scaled, 2 * q + t + 1 + 2)
                        dve.wait_ge(gated_ready, 2 * q + t + 1)
                        dve.tensor_tensor(hidden[:, t, :], hidden[:, t, :], gated[:, t, :], ALU.mult).then_inc(hidden_ready, 1)
                    for t in (0, 1):
                        dve.wait_ge(hid_hi, 2 * q + t + 1)
                        dve.tensor_tensor(y_lo[:, t, :], hidden[:, t, :], y_hi[:, t, :].bitcast(fp32),
                                          ALU.subtract).then_inc(hid_lo, 1)

                def add_down(u, q, m):
                    done(u.tile + m)
                    dve.wait_ge(ffn_x, 8 * q + m + 1)
                    dve.scalar_tensor_tensor(xs[:, m, :], AB[m % 4][:, :], 0.5, xs[:, m, :], ALU.mult, ALU.add).then_inc(ffn_x, 1)

                split(unit(l, base + 1))
                norm_factor(N)
                dve.wait_ge(r_ready, N + 1)
                gates(unit(l, base), q0)
                split(unit(l, base + 2))
                ups(unit(l, base + 1), q0)
                with dve.Fori(0, PAIRS) as i:
                    for j in (0, 1):
                        at = lambda k: unit(l, base + 2 + 3 * j + k, i, 6, 24)
                        q = q0 + 2 * i + j
                        split(at(1))
                        for m in range(KT):
                            add_down(at(0), q, m)
                        split(at(2))
                        gates(at(1), q + 1)
                        split(unit(l, base + 2 + 3 * j + 3, i, 6, 24))
                        ups(at(2), q + 1)
                if f == 0:
                    split(unit(l, base + 33))
                for m in range(KT):
                    add_down(unit(l, base + 32), q0 + GROUPS - 1, m)
                    if norm_after is not None and m:
                        gained_lo(norm_after, 1, m - 1)
                if norm_after is not None:
                    gained_lo(norm_after, 1, KT - 1)
                    add_squares(norm_after)

            def dil_softmax(H, b):
                if b == 0:
                    dve.wait_ge(bias_landed, 16 * H + 16)
                dve.wait_ge(dil_s, 4 * H + b + 1)
                for g, (c, n, bank, at, off) in enumerate(((0, 4 * P, AB[0], 0, (3 - b) * P), (4 * P, P, AB[1], 0, NC * P),
                                                           (5 * P, P, AB[1], P, (NC + 1) * P))):
                    q = 2 * g * NB + b
                    dve.scalar_tensor_tensor(s_sb[:, c:c + n], bank[:, at:at + n], rqk[:, q:q + 1], bias_f[:, off:off + n],
                                             ALU.mult, ALU.add).then_inc(dil_biased, 1)
                dve.wait_ge(dil_biased, 12 * H + 3 * b + 3 + FREE)
                dve.tensor_reduce(row_max[:, :], s_sb, axis=AX.X, op=ALU.max).then_inc(dil_max, 1)
                dve.wait_ge(dil_max, 8 * H + 2 * b + 1)
                dve.tensor_scalar(neg_max[:, :], row_max[:, :], -1.0, None, ALU.mult).then_inc(dil_max, 1)

            def dil_divide(H, b):
                dve.wait_ge(dil_exp, 4 * H + b + 1)
                dve.reciprocal(rden[:, :], den[:, :]).then_inc(dil_recip, 1)
                dve.wait_ge(dil_recip, 4 * H + b + 1)
                dve.tensor_scalar(s_sb, s_sb, rden[:, 0:1], None, ALU.mult).then_inc(dil_p, 1)

            def dil_copy(H, b):
                dve.wait_ge(dil_t, 4 * H + b + 1)
                dve.wait_ge(dil_pv, 4 * H + b + FREE)
                dve.tensor_copy(p_t[:, 4 * P:6 * P], AB[1][:, 2 * P:4 * P]).then_inc(dil_t_dve, 1)

            def dil_out(H, j):
                dve.wait_ge(dil_hi, H + 1)
                dve.tensor_tensor(y_lo[:, ds(8 + j, 1), :], AB[3][:, :].unsqueeze(1),
                                  y_hi[:, ds(8 + j, 1), :].bitcast(fp32), ALU.subtract).then_inc(dil_lo, 1)

            def rope(H, i):
                dve.wait_ge(swapped, 4 * H + 2 * i + 2)
                dve.tensor_tensor(rope_c, PB[i][:, :], cos_r[:, :], ALU.mult).then_inc(rope_step, 1)
                dve.tensor_tensor(swap, swap, sin_r[:, :], ALU.mult).then_inc(rope_step, 1)
                dve.wait_ge(rope_step, 6 * H + 3 * i + 2)
                dve.tensor_tensor(xs[:, 6 + i, :], rope_c, swap, ALU.add).then_inc(rope_step, 1)

            def ret_decay(H, a):
                dve.wait_ge(ret_s, 4 * H + a + 1)
                if a >= 2:
                    dve.wait_ge(ret_pv, 4 * H + a - 1)
                dve.scalar_tensor_tensor(ret_pt[a % 2], AB[0][:, :], RET_DK ** -0.5, decay_f[:, (3 - a) * P:(7 - a) * P],
                                         ALU.mult, ALU.mult).then_inc(ret_p, 1)

            def heads(l, n, prev, first=None):
                H = 4 * l + n
                at = lambda k: unit(l, HEAD_BASE + k, n, 8, 19)
                T = at(0).tile
                split(at(1))
                if first is not None:
                    norm_factor(first)
                    dve.wait_ge(norm_newton, 3 * first + 3)
                    dve.tensor_copy(r6[:, :].rearrange("p (t b) -> p t b", b=NB),
                                    r_col[:, :].unsqueeze(1).to_broadcast([P, 6, NB])).then_inc(r6_ready, 1)
                    dve.wait_ge(r6_ready, 2 * l + 1)
                    dve.tensor_tensor(rr6[:, :], r6[:, :], r6[:, :], ALU.mult).then_inc(r6_ready, 1)
                    dve.wait_ge(r_ready, first + 1)
                    dve.tensor_tensor(cos_r[:, :], cos_t[:, :], r_b[:, :], ALU.mult).then_inc(rope_tables, 1)
                    dve.tensor_tensor(sin_r[:, :], sin_t[:, :], r_b[:, :], ALU.mult).then_inc(rope_tables, 1)
                    dve.wait_ge(rope_tables, 2 * l + 2)
                    dve.wait_ge(x_spilled, 16 * (l + 1))
                rope(H, 0)
                if prev:
                    dil_softmax(H - 1, 0)
                    dil_divide(H - 1, 0)
                rope(H, 1)
                if prev:
                    dil_copy(H - 1, 0)
                split(at(2))
                if prev:
                    dil_softmax(H - 1, 1)
                    dil_divide(H - 1, 1)
                    dil_copy(H - 1, 1)
                    dil_softmax(H - 1, 2)
                    dil_divide(H - 1, 2)
                split(at(3))
                done(T + 6)
                dve.tensor_tensor(silu[:, 0, :], PB[2][:, :], r_b[:, :], ALU.mult).then_inc(rg_scaled, 1)
                if prev:
                    dil_copy(H - 1, 2)
                done(T + 7)
                dve.tensor_tensor(silu[:, 1, :], PB[3][:, :], r_b[:, :], ALU.mult).then_inc(rg_scaled, 1)
                if prev:
                    dil_softmax(H - 1, 3)
                    dil_divide(H - 1, 3)
                for e in (0, 1):
                    dve.wait_ge(rg_sig, 2 * H + e + 1)
                    dve.tensor_tensor(silu[:, e, :], silu[:, e, :], work[:, 10 + e, :], ALU.mult).then_inc(silu_ready, 1)
                if prev:
                    dil_copy(H - 1, 3)
                split(at(4))
                if prev:
                    dil_out(H - 1, n - 1)
                dve.wait_ge(decay_landed, 16 * H + 16)
                ret_decay(H, 0)
                split(at(5))
                ret_decay(H, 1)
                ret_decay(H, 2)
                split(at(6), 1024)
                ret_decay(H, 3)
                split(at(7))
                done(T + 14)
                dve.tensor_tensor(v2_t, PB[2][:, :], r_b[:, :], ALU.mult).then_inc(v2_scaled, 1)
                dve.wait_ge(ret_sum, H + 1)
                dve.tensor_scalar(t_var[:, :], AB[0][:, 0:NB], 1.0 / RET_DV, EPS, ALU.mult, ALU.add).then_inc(ret_var, 1)
                dve.wait_ge(qk_sum, 6 * H + 6)
                dve.wait_ge(r6_ready, 2 * l + 2)
                dve.scalar_tensor_tensor(q_raw[:, :], AB[1][:, 0:NQ], 1.0 / DIL_DH, rr6[:, :], ALU.mult, ALU.mult).then_inc(qk_var, 1)
                dve.wait_ge(qk_var, 2 * H + 1)
                dve.tensor_scalar(q_var[:, :], q_raw[:, :], EPS, None, ALU.add).then_inc(qk_var, 1)
                dve.wait_ge(ret_exp, H + 1)
                newton(t_r, t_exp, t_a, t_b, t_var, ret_newton, 3 * H)
                dve.wait_ge(qk_exp, H + 1)
                newton(q_y, q_exp, q_a, q_b, q_var, qk_newton, 4 * H)
                dve.wait_ge(qk_newton, 4 * H + 3)
                dve.tensor_tensor(rqk[:, :], q_y[:, :], r6[:, :], ALU.mult).then_inc(qk_newton, 1)
                split(at(8))
                dve.wait_ge(ret_bcast, H + 1)
                for e in (0, 1):
                    dve.tensor_tensor(ret_og[e], ret_og[e], AB[3][:, :], ALU.mult).then_inc(ret_y, 1)
                for e in (0, 1):
                    dve.wait_ge(ret_y, 4 * H + 1 + e)
                    dve.tensor_tensor(ret_og[e], ret_og[e], silu[:, e, :], ALU.mult).then_inc(ret_y, 1)
                for g, bank in enumerate((AB[1], AB[0], AB[2])):
                    dve.wait_ge(k_bcast, 3 * H + g + 1)
                    dve.tensor_tensor(xs[:, 2 * g + 1, :], xs[:, 2 * g + 1, :], bank[:, :], ALU.mult).then_inc(k_scaled, 1)
                for e in (0, 1):
                    dve.wait_ge(ret_hi, 2 * H + e + 1)
                    dve.tensor_tensor(y_lo[:, ds(2 * n + e, 1), :], ret_og[e].unsqueeze(1),
                                      y_hi[:, ds(2 * n + e, 1), :].bitcast(fp32), ALU.subtract).then_inc(ret_lo, 1)

            def merge(l):
                def gates(u, M):
                    for t in (0, 1):
                        done(u.tile + t)
                        dve.tensor_tensor(gate_s[:, t, :], PB[t][:, :], r_b[:, :], ALU.mult).then_inc(mg_scaled, 1)

                def merged(u, M):
                    for t in (0, 1):
                        done(u.tile + t)
                        dve.wait_ge(mg_sig, 2 * M + t + 1)
                        dve.tensor_tensor(gated[:, t, :], PB[2 + t][:, :], sig[:, t, :], ALU.mult).then_inc(mg_y, 1)
                    dve.wait_ge(mg_y, 2 * M + 2 + 2)
                    dve.tensor_tensor(work[:, 6, :], gated[:, 0, :], gated[:, 1, :], ALU.add).then_inc(mg_sum, 1)
                    dve.wait_ge(mg_hi_ready, M + 1)
                    dve.tensor_tensor(mg_lo[:, :], work[:, 6, :], mg_hi[:, :].bitcast(fp32), ALU.subtract).then_inc(mg_lo_ready, 1)

                def add_out(u, M, m):
                    done(u.tile + m)
                    dve.wait_ge(mix_x, 8 * M + m + 1)
                    dve.tensor_tensor(xs[:, m, :], AB[m % 4][:, :], xs[:, m, :], ALU.add).then_inc(mix_x, 1)

                M0 = KT * l
                split(unit(l, MERGE_BASE + 1), 1536)
                gates(unit(l, MERGE_BASE), M0)
                split(unit(l, MERGE_BASE + 2), 1024)
                dve.wait_ge(x_restored, 16 * (l + 1))
                merged(unit(l, MERGE_BASE + 1), M0)
                with dve.Fori(0, 3) as i:
                    for j in (0, 1):
                        at = lambda k: unit(l, MERGE_BASE + 2 + 3 * j + k, i, 6, 24)
                        M = M0 + 2 * i + j
                        split(at(1))
                        for m in range(KT):
                            add_out(at(0), M, m)
                        split(at(2), 1536)
                        gates(at(1), M + 1)
                        split(unit(l, MERGE_BASE + 5 + 3 * j, i, 6, 24), 1024)
                        merged(at(2), M + 1)
                split(unit(l, MERGE_BASE + 21))
                for m in range(KT):
                    add_out(unit(l, MERGE_BASE + 20), M0 + 6, m)
                split(unit(l, MERGE_BASE + 22), 1536)
                gates(unit(l, MERGE_BASE + 21), M0 + 7)
                split(unit(l, MERGE_BASE + 23), 1024)
                merged(unit(l, MERGE_BASE + 22), M0 + 7)
                split(unit(l, MERGE_BASE + 24))
                for m in range(KT):
                    add_out(unit(l, MERGE_BASE + 23), M0 + 7, m)
                    if m:
                        gained_lo(3 * l + 2, 2, m - 1)
                gained_lo(3 * l + 2, 2, KT - 1)
                add_squares(3 * l + 2)

            dve.sem_inc(weights_lo, LO_CREDIT)
            for s in (gate_scaled, up_scaled, mg_scaled, mg_y):
                dve.sem_inc(s, 2)
            for s in (ret_p, dil_biased, ret_lo, dil_t_dve, dil_lo, h_lo_ready):
                dve.sem_inc(s, FREE)
            dve.sem_inc(mix_x, 8)
            dve.memset(ones[:, :], 1.0).then_inc(ones_set, 1)
            dve.memset(relb[N_BUCKETS:N_BUCKETS + 1, :], 1.0).then_inc(relb_one, 1)
            dve.wait_ge(dexp_t, 1)
            dve.tensor_copy(d_e[:, :], AB[1][0:56, 0:2]).then_inc(dstep, 1)
            dve.wait_ge(params_t, 1)
            dve.tensor_copy(params[:, :], AB[0][:, 0:DEPTH * ROWS]).then_inc(params_ready, 1)
            steps = [2]

            def chain(ins):
                ins.then_inc(dstep, 1)
                dve.wait_ge(dstep, steps[0])
                steps[0] += 1

            dve.wait_ge(d_exp, 1)
            chain(dve.tensor_scalar(d_w[:, :], d_y[:, :], -1.0, 1.0, ALU.mult, ALU.add))
            chain(dve.tensor_scalar(d_d[:, :], d_y[:, :], -1.0, 2.0, ALU.mult, ALU.add))
            chain(dve.reciprocal(d_d[:, :], d_d[:, :]))
            chain(dve.tensor_tensor(d_s[:, :], d_y[:, :], d_d[:, :], ALU.mult))
            chain(dve.tensor_tensor(d_s2[:, :], d_s[:, :], d_s[:, :], ALU.mult))
            chain(dve.tensor_scalar(d_p[:, :], d_s2[:, :], 1.0 / 19, 1.0 / 17, ALU.mult, ALU.add))
            for odd in range(15, 0, -2):
                chain(dve.tensor_tensor(d_p[:, :], d_p[:, :], d_s2[:, :], ALU.mult))
                chain(dve.tensor_scalar(d_p[:, :], d_p[:, :], 1.0 / odd, None, ALU.add))
            chain(dve.tensor_tensor(d_p[:, :], d_p[:, :], d_s[:, :], ALU.mult))
            chain(dve.tensor_scalar(d_lg[:, :], d_p[:, :], -2.0, None, ALU.mult))
            chain(dve.tensor_scalar(d_m[:, :], d_y[:, :], 0.5, None, ALU.is_gt))
            dve.wait_ge(d_log, 1)
            chain(dve.tensor_tensor(d_ln[:, :], d_ln[:, :], d_lg[:, :], ALU.subtract))
            chain(dve.tensor_tensor(d_ln[:, :], d_ln[:, :], d_m[:, :], ALU.mult))
            chain(dve.tensor_tensor(d_lg[:, :], d_lg[:, :], d_ln[:, :], ALU.add))
            chain(dve.tensor_scalar(dpos, dist, 0.0, d_lg[:, 0:1], ALU.max, ALU.mult))
            chain(dve.tensor_scalar(dneg, dist, 0.0, d_lg[:, 1:2], ALU.min, ALU.mult))
            dve.tensor_tensor(dpos, dpos, dneg, ALU.subtract).then_inc(d_log, 1)
            for c, bank in enumerate((PB[0], PB[1], PB[2], PB[3], AB[2])):
                w = min(512, NT * WD - 512 * c)
                dve.wait_ge(bias_mm, c + 1)
                dve.tensor_copy(bdiag[:, 512 * c:512 * c + w], bank[0:12, 0:w]).then_inc(bias_evicted, 1)
            for m in range(KT):
                dve.wait_ge(x_transposed, m + 1)
                dve.tensor_copy(xs[:, m, :], PB[m % 4][:, :]).then_inc(ffn_x, 1)
            with dve.Fori(0, DEPTH) as l:
                split(unit(l, 0))
                dve.wait_ge(par_ready, 2 * l + 2)
                for m in range(KT):
                    gained_lo(3 * l, 0, m)
                add_squares(3 * l)
                ffn(l, 0, 3 * l + 1)
                heads(l, 0, False, 3 * l + 1)
                with dve.Fori(1, RET_HEADS) as n:
                    heads(l, n, True)
                for b in range(NB):
                    dil_softmax(4 * l + 3, b)
                    dil_divide(4 * l + 3, b)
                    dil_copy(4 * l + 3, b)
                dil_out(4 * l + 3, 3)
                merge(l)
                ffn(l, 1, None)
            for n in range(8):
                dve.wait_ge(out_turned, n + 1)
                dve.tensor_copy(x_tok[:, n // 2, (n % 2) * 512:(n % 2) * 512 + 512], AB[n % 4][:, :]).then_inc(out_copied, 1)


def rope_tables():
    half = RET_DK // 2
    inv = np.float32(10000.0) ** (-np.arange(half, dtype=np.float32) / np.float32(half))
    tau = np.arange(SEQ)
    t = (4 * (tau % P) + tau // P).astype(np.float32)
    ang = (t[None, :] * inv.astype(np.float32)[:, None]).astype(np.float32)
    cos, sin = np.cos(ang).astype(np.float32), np.sin(ang).astype(np.float32)
    return np.concatenate([cos, cos]), np.concatenate([-sin, sin])


def bias_selection():
    sel = np.zeros((N_BUCKETS + 1, NT, WD), np.float32)
    nb = N_BUCKETS // 2
    for c in range(NT):
        for w in range(WD):
            step = w - (P - 1)
            rel = 4 * step + (c - 3 if c < NC else 0)
            valid = (abs(rel) <= 64, abs(step) <= 64, step % 4 == 0)[0 if c < NC else c - NC + 1]
            n = abs(rel)
            if n >= nb // 2:
                exact = nb // 2
                big = exact + int(np.float32(np.log(np.float32(n) / np.float32(exact))) / np.float32(math.log(MAX_DISTANCE / exact))
                                  * np.float32(nb - exact))
                n = min(big, nb - 1)
            sel[(nb if rel > 0 else 0) + n, c, w] = 1.0
            sel[N_BUCKETS, c, w] = 0.0 if valid else NEG
    return sel.reshape(N_BUCKETS + 1, NT * WD)


def token_distances():
    w = np.arange(WD)[None, :] - (P - 1)
    d = (4 * w + (np.arange(NC)[:, None] - 3)).astype(np.float32)
    return np.tile(d, (DEPTH * RET_HEADS, 1))


def constants():
    cos, sin = rope_tables()
    return {"c_ident": np.eye(P, dtype=np.float32), "c_cos": cos, "c_sin": sin, "c_onehot": bias_selection(),
            "c_dist": token_distances(), "c_sel": np.repeat(np.eye(DEPTH * RET_HEADS, dtype=np.float32), NC, axis=1)}


_INS = ["x", "rel_bias", "norm_ffn1", "ffn1_gate", "ffn1_up", "ffn1_down", "norm_mix", "w_in", "b_gate", "ret_decay_exp",
        "ret_norm", "w_ret_o", "dil_q_norm", "dil_k_norm", "w_dil_o", "w_out", "norm_ffn2", "ffn2_gate", "ffn2_up",
        "ffn2_down"]


def kernel(**inputs):
    import concourse.bacc as bacc
    from concourse.bass_utils import run_bass_kernel_spmd

    nc = bacc.Bacc("TRN2", target_bir_lowering=False, num_devices=1)
    arrays = {f"in_{k}": np.ascontiguousarray(inputs[k]) for k in _INS}
    arrays.update(constants())
    args = {k.removeprefix("in_"): nc.dram_tensor(k, a.shape, mybir.dt.from_np(a.dtype), kind="ExternalInput").ap()
            for k, a in arrays.items()}
    out = nc.dram_tensor("out", (SEQ, D_MODEL), mybir.dt.float32, kind="ExternalOutput").ap()
    build(nc, out=out, **args)
    r = run_bass_kernel_spmd(nc, [arrays], core_ids=[0])
    return r.results[0]["out"].reshape(1, SEQ, D_MODEL)
```

```python
import math
from typing import NamedTuple

import numpy as np
import concourse.bass as bass
from concourse import mybir
from contextlib import ExitStack

P = 128
SEQ, D_MODEL, DEPTH, D_FF = 512, 1024, 2, 2816
RET_HEADS, RET_DK, RET_DV = 4, 128, 256
DIL_GROUPS, DIL_HPG, DIL_DH = 3, 4, 128
N_BUCKETS, MAX_DISTANCE, EPS, NEG = 32, 1024, 1e-6, -1e30
KT = D_MODEL // P
NB = SEQ // P
C_RQ, C_RK, C_RV, C_RG = 0, 512, 1024, 2048
C_DQ, C_DK, C_DV, C_GR, C_GD = 3072, 4608, 6144, 7680, 8704
GRP = 256
GROUPS = D_FF // GRP
PAIRS = (GROUPS - 1) // 2
NC, NT, WD = 2 * NB - 1, 2 * NB + 1, 2 * P
R_N = (0, 8, 16)
R_BG, R_RN, R_QN, R_KN, ROWS = 24, 40, 48, 49, 50


class Unit(NamedTuple):
    index: object
    slot: int
    turn: object
    tile: object
    before: int


FFN_TILES = [2, 2] + [2, 2, 8] * (GROUPS - 1) + [8]
HEAD_TILES = [2, 4, 2, 2, 2, 2, 1, 4]
MERGE_TILES = [2, 1, 1, 1, 1, 2, 8] + [2, 2, 8] * (KT - 2) + [8]
TILES = FFN_TILES + HEAD_TILES * RET_HEADS + MERGE_TILES + FFN_TILES
FFN_BASE = (0, len(FFN_TILES) + len(HEAD_TILES) * RET_HEADS + len(MERGE_TILES))
HEAD_BASE = len(FFN_TILES)
MERGE_BASE = HEAD_BASE + len(HEAD_TILES) * RET_HEADS
UNITS_LAYER, TILES_LAYER = len(TILES), sum(TILES)
FIRST_CREDIT = 9
FREE = 1
LO_CREDIT = 2


def unit(layer, fixed, loop=0, loop_units=0, loop_tiles=0):
    return Unit(layer * UNITS_LAYER + loop * loop_units + fixed, fixed % 2,
                layer * (UNITS_LAYER // 2) + loop * (loop_units // 2) + fixed // 2,
                layer * TILES_LAYER + loop * loop_tiles + sum(TILES[:fixed]), TILES[fixed - 1])


def build(nc, x, rel_bias, norm_ffn1, ffn1_gate, ffn1_up, ffn1_down, norm_mix, w_in, b_gate, ret_decay_exp,
          ret_norm, w_ret_o, dil_q_norm, dil_k_norm, w_dil_o, w_out, norm_ffn2, ffn2_gate, ffn2_up, ffn2_down,
          c_ident, c_cos, c_sin, c_onehot, c_dist, c_sel, out):
    fp32, f32r = mybir.dt.float32, mybir.dt.float32r
    ALU, ACT, AX = mybir.AluOpType, mybir.ActivationFunctionType, mybir.AxisListType
    ds = bass.ds

    x_spill = nc.dram_tensor("x_spill", [P, KT, SEQ], fp32, kind="Internal").ap()
    bias_diag = nc.dram_tensor("bias_diag", [DIL_GROUPS * DIL_HPG, NT * WD], fp32, kind="Internal")
    bias_full = nc.dram_tensor("bias_full", [P, DIL_HPG, NT, P], fp32, kind="Internal").ap()
    decay_diag = nc.dram_tensor("decay_diag", [DEPTH * RET_HEADS * NC, WD], fp32, kind="Internal")
    decay_full = nc.dram_tensor("decay_full", [P, DEPTH * RET_HEADS, NC, P], fp32, kind="Internal").ap()

    rows = "l (k p) c -> p l k c"
    win_v, reto_v, dilo_v, wout_v = (w.rearrange(rows, p=P) for w in (w_in, w_ret_o, w_dil_o, w_out))
    gate_v = [w.rearrange(rows, p=P) for w in (ffn1_gate, ffn2_gate)]
    up_v = [w.rearrange(rows, p=P) for w in (ffn1_up, ffn2_up)]
    down_v = [w.rearrange(rows, p=P) for w in (ffn1_down, ffn2_down)]

    ctx = ExitStack()
    with ctx:
        def sb(name, shape, dt=fp32):
            return ctx.enter_context(nc.sbuf_tensor(name, shape, dt))

        def sem(name):
            return ctx.enter_context(nc.semaphore(name))

        raw = sb("raw", [P, 2, 2048])
        w_hi = sb("w_hi", [P, 2, 2048], f32r)
        w_lo = sb("w_lo", [P, 2, 2048], f32r)
        xs = sb("xs", [P, KT, SEQ])
        h_hi = sb("h_hi", [P, KT, SEQ], f32r)
        h_lo = sb("h_lo", [P, KT, SEQ], f32r)
        y_hi = sb("y_hi", [P, 12, SEQ], f32r)
        y_lo = sb("y_lo", [P, 12, SEQ], f32r)
        mg_hi = sb("mg_hi", [P, 2, SEQ], f32r)
        mg_lo = sb("mg_lo", [P, 2, SEQ], f32r)
        ret_v_hi = sb("ret_v_hi", [P, NB, RET_DV], f32r)
        r_b = sb("r_b", [P, SEQ])
        cos_r = sb("cos_r", [P, SEQ])
        sin_r = sb("sin_r", [P, SEQ])
        bias_sb = sb("bias_sb", [P, 1, NT, P])
        decay_sb = sb("decay_sb", [P, 1, NC, P])
        bias_f = bias_sb[:, :, :, :].rearrange("p o c i -> p (o c i)")
        decay_f = decay_sb[:, :, :, :].rearrange("p o c i -> p (o c i)")
        ident = sb("ident", [P, P])
        ones = sb("ones", [P, 2])
        params = sb("params", [P, DEPTH * ROWS])
        par = sb("par", [P, ROWS])
        gq = sb("gq", [P, 1])
        work = sb("work", [P, 16, SEQ])
        flat = work[:, :, :].rearrange("p t n -> p (t n)")

        def tiny(name, n=NB):
            return sb(name, [P, n])

        n_var, n_ln, n_exp, n_a, n_b, r_col = (tiny(f"n_{k}") for k in ("var", "ln", "exp", "a", "b", "r"))
        t_var, t_ln, t_exp, t_a, t_b, t_r = (tiny(f"t_{k}") for k in ("var", "ln", "exp", "a", "b", "r"))
        NQ = 2 * DIL_GROUPS * NB
        q_raw, q_var, q_ln, q_exp, q_a, q_b, q_y, rqk, r6, rr6 = (
            tiny(f"q_{k}", NQ) for k in ("raw", "var", "ln", "exp", "a", "b", "y", "rqk", "r6", "rr6"))
        row_max, neg_max, den, rden = (tiny(k, 1) for k in ("row_max", "neg_max", "den", "rden"))
        relb = sb("relb", [N_BUCKETS + 1, 12])
        sel = sb("sel", [8, 56])
        dexp = sb("dexp", [8, 2])
        d_e, d_y, d_w, d_ln, d_d, d_s, d_s2, d_p, d_lg, d_m = (
            sb(f"d_{k}", [56, 2]) for k in ("e", "y", "w", "ln", "d", "s", "s2", "p", "lg", "m"))

        PB = [ctx.enter_context(nc.psum_tensor(f"proj{i}", [P, SEQ], fp32)) for i in range(4)]
        AB = [ctx.enter_context(nc.psum_tensor(f"acc{i}", [P, SEQ], fp32)) for i in range(4)]

        y_hi_flat, y_lo_flat = (y[:, :, :].rearrange("p t n -> p (t n)") for y in (y_hi, y_lo))

        def pt_split(y_flat, n, a):
            return y_flat[:, ds((2 * n + a % 2) * SEQ, SEQ)]

        def q_split(y_flat, n):
            return y_flat[:, ds((8 + n) * SEQ, SEQ)]

        k_hi, k_lo, v_lo = mg_hi[:, 1, :], mg_lo[:, 1, :], (mg_hi[:, 0, :], mg_lo[:, 0, :])

        gate_s, sig, gated, hidden = (work[:, 2 * i:2 * i + 2, :] for i in range(4))
        n_sq, ssq = [work[:, 10, :], work[:, 11, :]], work[:, 12, :]
        ret_v = work[:, 0:2, :].rearrange("p t (b n) -> p (t b) n", n=RET_DV)
        silu = work[:, 2:4, :]
        dil_v = work[:, 4:7, :].rearrange("p g (b n) -> p g b n", n=P)
        s_sb = flat[:, 7 * SEQ:7 * SEQ + 768]
        p_t = flat[:, 7 * SEQ + 768:10 * SEQ]
        ret_pt = [work[:, 7, :], work[:, 8, :]]
        swap, rope_c = work[:, 10, :], work[:, 11, :]
        qk_sq = [work[:, 12, :], work[:, 13, :]]
        ret_og = [work[:, 10, :], work[:, 11, :]]
        ret_sq = [work[:, 9, :], work[:, 14, :]]
        v2_t = work[:, 15, :]
        mg_gate, mg_sigm = [work[:, 0:2, :], work[:, 10:12, :]], [work[:, 2:4, :], work[:, 12:14, :]]
        mg_prod, merged_t = work[:, 14:16, :], work[:, 14, :]
        x_tok = work[:, 0:8, :].rearrange("p t n -> p (t n)").rearrange("p (r d) -> p r d", r=NB)
        onehot = xs[0:N_BUCKETS + 1, 0:5, :].rearrange("p t n -> p (t n)")[:, 0:NT * WD]
        bdiag = [work[0:12, t, :] for t in (8, 9, 13, 14, 15)]
        prow = work[0:DEPTH * ROWS, 10, 0:P]
        dist, dneg, dpos = cos_r[0:56, 0:WD], cos_r[0:56, WD:2 * WD], sin_r[0:56, 0:WD]

        ident_in, x_in, ones_set = sem("ident_in"), [sem("x_in0"), sem("x_in1")], sem("ones_set")
        bias_in, decay_in, dist_in, params_in, rope_in = (
            sem(k) for k in ("bias_in", "decay_in", "dist_in", "params_in", "rope_in"))
        relb_one = sem("relb_one")
        params_t, params_ready, dexp_t = sem("params_t"), sem("params_ready"), sem("dexp_t")
        bias_mm, bias_evicted, x_transposed = sem("bias_mm"), sem("bias_evicted"), sem("x_transposed")
        dstep, d_exp, d_log, decay_done = sem("dstep"), sem("d_exp"), sem("d_log"), sem("decay_done")
        bias_out, decay_out, bias_exp, decay_exp = (sem(k) for k in ("bias_out", "decay_out", "bias_exp", "decay_exp"))
        raw_landed = [sem("raw_landed0"), sem("raw_landed1")]
        weights_hi, weights_lo, tiles_done = sem("weights_hi"), sem("weights_lo"), sem("tiles_done")
        par_ready, h_hi_ready, h_lo_ready = sem("par_ready"), sem("h_hi_ready"), sem("h_lo_ready")
        x_squared, ssq_added, norm_sum, norm_var = (sem(k) for k in ("x_squared", "ssq_added", "norm_sum", "norm_var"))
        norm_ln, norm_exp, norm_newton, norm_bcast = (sem(k) for k in ("norm_ln", "norm_exp", "norm_newton", "norm_bcast"))
        r_ready, rope_tables, r6_ready = sem("r_ready"), sem("rope_tables"), sem("r6_ready")
        gate_scaled, sig_ready, gated_ready, up_scaled = (sem(k) for k in ("gate_scaled", "sig_ready", "gated_ready", "up_scaled"))
        hidden_ready, hid_hi, hid_lo, ffn_x = (sem(k) for k in ("hidden_ready", "hid_hi", "hid_lo", "ffn_x"))
        x_spilled, x_restored = sem("x_spilled"), sem("x_restored")
        decay_landed, bias_landed = sem("decay_landed"), sem("bias_landed")
        swapped, rope_step, ret_v_ready, rg_scaled = (sem(k) for k in ("swapped", "rope_step", "ret_v_ready", "rg_scaled"))
        rg_sig, silu_ready, ret_s, ret_p, ret_pv = (sem(k) for k in ("rg_sig", "silu_ready", "ret_s", "ret_p", "ret_pv"))
        ret_o_read, ret_sum, ret_var, ret_ln, ret_exp, ret_newton, ret_bcast = (
            sem(k) for k in ("ret_o_read", "ret_sum", "ret_var", "ret_ln", "ret_exp", "ret_newton", "ret_bcast"))
        ret_sq_added, ret_qk_hi, ret_qk_lo, ret_pt_hi, ret_pt_lo, ret_v_hi_ready, ret_v_lo_ready = (
            sem(k) for k in ("ret_sq_added", "ret_qk_hi", "ret_qk_lo", "ret_pt_hi", "ret_pt_lo", "ret_v_hi_ready",
                             "ret_v_lo_ready"))
        ret_y, ret_hi, ret_lo = sem("ret_y"), sem("ret_hi"), sem("ret_lo")
        qk_squared, qk_sum, qk_var, qk_ln, qk_exp, qk_newton = (
            sem(k) for k in ("qk_squared", "qk_sum", "qk_var", "qk_ln", "qk_exp", "qk_newton"))
        k_bcast, k_scaled, v01_ready, v2_scaled, v2_turned, v2_ready = (
            sem(k) for k in ("k_bcast", "k_scaled", "v01_ready", "v2_scaled", "v2_turned", "v2_ready"))
        dil_s, dil_biased, dil_max, dil_exp, dil_recip, dil_p = (
            sem(k) for k in ("dil_s", "dil_biased", "dil_max", "dil_exp", "dil_recip", "dil_p"))
        dil_t, dil_t_act, dil_t_dve, dil_pv, dil_hi, dil_lo = (
            sem(k) for k in ("dil_t", "dil_t_act", "dil_t_dve", "dil_pv", "dil_hi", "dil_lo"))
        mg_scaled, mg_sig, mg_y, mg_sum, mg_hi_ready, mg_lo_ready, mix_x = (
            sem(k) for k in ("mg_scaled", "mg_sig", "mg_y", "mg_sum", "mg_hi_ready", "mg_lo_ready", "mix_x"))
        out_turned, out_copied, stored = sem("out_turned"), sem("out_copied"), sem("stored")

        block = ctx.enter_context(nc.Block())

        @block.sync
        def _(sp):
            def load(u, parts):
                sp.wait_ge(weights_lo, u.index + 1)
                for dst, src in parts:
                    sp.dma_start(dst, src).then_inc(raw_landed[u.slot], 16)

            def slot(u, n=2048):
                return raw[:, u.slot:u.slot + 1, 0:n]

            def cols256(u, w, layer, col):
                v = slot(u).rearrange("p o (k c) -> p o k c", c=2 * P)
                load(u, [(v[:, :, k:k + 4, :], w[:, ds(layer, 1), k:k + 4, ds(col, 2 * P)]) for k in (0, 4)])

            def two_cols128(u, w, layer, col0, col1):
                v = slot(u).rearrange("p o (k c) -> p o k c", c=2 * P)
                load(u, [(v[:, :, :, 0:P], w[:, ds(layer, 1), :, ds(col0, P)]),
                         (v[:, :, :, P:2 * P], w[:, ds(layer, 1), :, ds(col1, P)])])

            def cols128(u, w, layer, col, kt):
                v = slot(u, kt * P).rearrange("p o (k c) -> p o k c", c=P)
                load(u, [(v[:, :, k:k + kt // 2, :], w[:, ds(layer, 1), k:k + kt // 2, ds(col, P)]) for k in (0, kt // 2)])

            def down_rows(u, w, layer, g):
                v = slot(u).rearrange("p o (k c) -> p o k c", c=D_MODEL)
                load(u, [(v[:, :, t:t + 1, :], w[:, ds(layer, 1), ds(2 * g + t, 1), :]) for t in (0, 1)])

            def ffn(l, f):
                base = FFN_BASE[f]
                cols256(unit(l, base), gate_v[f], l, 0)
                cols256(unit(l, base + 1), up_v[f], l, 0)
                with sp.Fori(0, PAIRS) as i:
                    for j in (0, 1):
                        at = lambda k: unit(l, base + 2 + 3 * j + k, i, 6, 24)
                        cols256(at(0), gate_v[f], l, (2 * i + j + 1) * GRP)
                        cols256(at(1), up_v[f], l, (2 * i + j + 1) * GRP)
                        down_rows(at(2), down_v[f], l, 2 * i + j)
                down_rows(unit(l, base + 32), down_v[f], l, GROUPS - 1)

            def head_units(l, n):
                at = lambda k: unit(l, HEAD_BASE + k, n, 8, 19)
                two_cols128(at(0), win_v, l, C_RQ + n * P, C_RK + n * P)
                cols256(at(1), win_v, l, C_RV + n * RET_DV)
                sp.wait_ge(ret_p, 4 * (4 * l + n) + FREE)
                sp.dma_start(decay_sb[:, :, :, :], decay_full[:, ds(4 * l + n, 1), :, :]).then_inc(decay_landed, 16)
                cols256(at(2), win_v, l, C_RG + n * RET_DV)
                for g in range(DIL_GROUPS):
                    col = 4 * g * P + n * P
                    two_cols128(at(3 + g), win_v, l, C_DQ + col, C_DK + col)
                cols128(at(6), win_v, l, C_DV + 8 * P + n * P, KT)
                two_cols128(at(7), win_v, l, C_DV + n * P, C_DV + 4 * P + n * P)
                sp.wait_ge(dil_biased, 12 * (4 * l + n) + FREE)
                sp.dma_start(bias_sb[:, :, :, :], bias_full[:, ds(n, 1), :, :]).then_inc(bias_landed, 16)

            def merge_gates(u, l, m):
                two_cols128(u, win_v, l, C_GR + m * P, C_GD + m * P)

            def merge_outs(u, l, m):
                v = slot(u, 1536).rearrange("p o (k c) -> p o k c", c=P)
                load(u, [(v[:, :, 0:8, :], reto_v[:, ds(l, 1), :, ds(m * P, P)]),
                         (v[:, :, 8:12, :], dilo_v[:, ds(l, 1), :, ds(m * P, P)])])

            def merge_wout(u, l, m):
                v = slot(u, 1024).rearrange("p o (k c) -> p o k c", k=1)
                load(u, [(v[:, :, :, c:c + 512], wout_v[:, ds(l, 1), ds(m, 1), c:c + 512]) for c in (0, 512)])

            row = 0
            for l in range(DEPTH):
                for w in (norm_ffn1, norm_mix, norm_ffn2, b_gate, ret_norm, dil_q_norm, dil_k_norm):
                    n = w.shape[1] // P
                    sp.dma_start(prow[row:row + n, :], w[l].rearrange("(m p) -> m p", p=P)).then_inc(params_in, 16)
                    row += n
            with sp.Fori(0, DEPTH) as l:
                ffn(l, 0)
                sp.wait_ge(decay_exp, 16 * DEPTH * RET_HEADS)
                sp.wait_ge(bias_exp, 16 * 2 * DIL_HPG)
                sp.dma_start(cos_r[:, :], c_cos).then_inc(rope_in, 16)
                sp.dma_start(sin_r[:, :], c_sin).then_inc(rope_in, 16)
                with sp.Fori(0, RET_HEADS) as n:
                    head_units(l, n)
                merge_gates(unit(l, MERGE_BASE), l, 0)
                cols128(unit(l, MERGE_BASE + 1), reto_v, l, 0, KT)
                cols128(unit(l, MERGE_BASE + 2), win_v, l, C_GR + P, KT)
                cols128(unit(l, MERGE_BASE + 3), win_v, l, C_GD + P, KT)
                cols128(unit(l, MERGE_BASE + 4), dilo_v, l, 0, DIL_HPG)
                merge_outs(unit(l, MERGE_BASE + 5), l, 1)
                sp.wait_ge(x_spilled, 16 * (l + 1))
                sp.wait_ge(dil_s, 16 * (l + 1))
                sp.dma_start(xs[:, :, :], x_spill).then_inc(x_restored, 16)
                merge_wout(unit(l, MERGE_BASE + 6), l, 0)
                with sp.Fori(0, 3) as i:
                    for j in (0, 1):
                        at = lambda k: unit(l, MERGE_BASE + 7 + 3 * j + k, i, 6, 24)
                        merge_gates(at(0), l, 2 * i + j + 2)
                        merge_outs(at(1), l, 2 * i + j + 2)
                        merge_wout(at(2), l, 2 * i + j + 1)
                merge_wout(unit(l, MERGE_BASE + 25), l, 7)
                ffn(l, 1)
            for half in (0, 1):
                c = slice(half * 512, (half + 1) * 512)
                sp.wait_ge(out_copied, NB * (half + 1))
                sp.dma_start(out.rearrange("(i r) d -> i r d", r=NB)[:, :, c], x_tok[:, :, c]).then_inc(stored, 16)
            sp.wait_ge(stored, 16 * 2)

        @block.gpsimd
        def _(pool):
            for l in range(DEPTH):
                pool.dma_start(dexp[4 * l:4 * l + 4, :], ret_decay_exp[l].rearrange("d h -> h d"),
                               allow_slow_non_contiguous=True).then_inc(decay_in, 16)
            pool.dma_start(sel[:, :], c_sel).then_inc(decay_in, 16)
            pool.dma_start(dist, c_dist).then_inc(dist_in, 16)
            pool.dma_start(relb[0:N_BUCKETS, :], rel_bias).then_inc(bias_in, 16)
            pool.dma_start(onehot, c_onehot).then_inc(bias_in, 16)
            pool.wait_ge(bias_evicted, 5)
            for c in range(5):
                w = min(512, NT * WD - 512 * c)
                pool.dma_start(bias_diag.ap()[:, 512 * c:512 * c + w], bdiag[c][:, 0:w]).then_inc(bias_out, 16)
            pool.wait_ge(decay_done, 1)
            pool.dma_start(decay_diag.ap(), dpos).then_inc(decay_out, 16)

            def add_squares(N):
                for m in range(1, KT):
                    pool.wait_ge(x_squared, KT * N + m + 1)
                    if m >= 2:
                        pool.wait_ge(ssq_added, (KT - 1) * N + m - 1)
                    pool.tensor_tensor(ssq, ssq, n_sq[m % 2], ALU.add).then_inc(ssq_added, 1)

            add_squares(0)
            pool.wait_ge(weights_hi, 3)
            pool.wait_ge(bias_out, 16 * 5)
            for j in range(DIL_HPG):
                first = bass.AP(bias_diag, j * NT * WD + P - 1, [[WD, NC], [-1, P], [1, P]])
                pool.dma_start(bias_full[:, j, 0:NC, :].rearrange("p c i -> c p i"), first).then_inc(bias_exp, 16)
                rest = bass.AP(bias_diag, (DIL_HPG + j) * NT * WD + NC * WD + P - 1,
                               [[DIL_HPG * NT * WD + WD, 2], [-1, P], [1, P]])
                pool.dma_start(bias_full[:, j, NC:NT, :].rearrange("p c i -> c p i"), rest).then_inc(bias_exp, 16)
            pool.wait_ge(decay_out, 16)
            for j in range(DEPTH * RET_HEADS):
                src = bass.AP(decay_diag, j * NC * WD + P - 1, [[WD, NC], [-1, P], [1, P]])
                pool.dma_start(decay_full[:, j, :, :].rearrange("p c i -> c p i"), src).then_inc(decay_exp, 16)

            def mix_and_ffn2(l):
                add_squares(3 * l + 1)
                with pool.Fori(0, RET_HEADS) as n:
                    pool.wait_ge(ret_o_read, 4 * (4 * l + n) + 2)
                    pool.tensor_tensor(ret_sq[0], ret_sq[0], ret_sq[1], ALU.add).then_inc(ret_sq_added, 1)
                add_squares(3 * l + 2)

            with pool.Fori(0, DEPTH - 1) as l:
                mix_and_ffn2(l)
                add_squares(3 * l + 3)
            mix_and_ffn2(DEPTH - 1)
            pool.wait_ge(bias_exp, 16 * 2 * DIL_HPG)
            pool.wait_ge(decay_exp, 16 * DEPTH * RET_HEADS)

        @block.tensor
        def _(pe):
            def three(o, s_hi, s_lo, m_hi, m_lo, start, stop):
                pe.matmul(o, s_hi, m_hi, start=start, stop=False)
                pe.matmul(o, s_hi, m_lo, start=False, stop=False)
                return pe.matmul(o, s_lo, m_hi, start=False, stop=stop)

            def begin(u):
                pe.wait_ge(weights_lo, u.index + 1 + LO_CREDIT)

            def tile_cols(u, bank, t, fresh=None, width=2 * P, between={}):
                for k in range(KT):
                    for step in between.get(k, ()):
                        step()
                    if fresh is not None:
                        pe.wait_ge(h_lo_ready, 8 * fresh + k + 1 + FREE)
                    c = k * width + t * P
                    last = three(bank[:, :], w_hi[:, u.slot, c:c + P], w_lo[:, u.slot, c:c + P],
                                 h_hi[:, k, :], h_lo[:, k, :], k == 0, k == KT - 1)
                last.then_inc(tiles_done, 1)

            def tile_tokens(u, bank, b):
                for k in range(KT):
                    c, t = k * 2 * P, slice(b * P, (b + 1) * P)
                    last = three(bank[:, 0:2 * P], h_hi[:, k, t], h_lo[:, k, t],
                                 w_hi[:, u.slot, c:c + 2 * P], w_lo[:, u.slot, c:c + 2 * P], k == 0, k == KT - 1)
                last.then_inc(tiles_done, 1)

            def norm_sums(N):
                pe.wait_ge(ssq_added, (KT - 1) * (N + 1))
                for b in range(NB):
                    last = pe.matmul(AB[0][:, b:b + 1], ssq[:, b * P:(b + 1) * P], ones[:, 0:1], start=True, stop=True)
                last.then_inc(norm_sum, 1)

            def spread(bank, col):
                for b in range(NB):
                    last = pe.matmul(bank[:, b * P:(b + 1) * P], col(b).to_broadcast([P, P]), ident[:, :],
                                     start=True, stop=True)
                return last

            def norm_spread(N):
                pe.wait_ge(norm_newton, 3 * N + 3)
                spread(AB[1], lambda b: r_col[:, b:b + 1]).then_inc(norm_bcast, 1)

            def ffn(l, f):
                base, q0, N = FFN_BASE[f], (2 * l + f) * GROUPS, 3 * l + 2 * f

                def gate(u, q, first=False):
                    begin(u)
                    for t in (0, 1):
                        pe.wait_ge(gate_scaled, 2 * q + t + 1)
                        tile_cols(u, PB[t], t, N if first else None)
                        if first:
                            (norm_sums, norm_spread)[t](N)

                def up(u, q, t):
                    pe.wait_ge(up_scaled, 2 * q + t + 1)
                    tile_cols(u, PB[2 + t], t)

                def down(u, q, half):
                    begin(u)
                    for m in range(KT):
                        pe.wait_ge(ffn_x, 8 * q + m + 5)
                        for t in (0, 1):
                            if m == 0:
                                pe.wait_ge(hid_lo, 2 * q + t + 1)
                            c = t * D_MODEL + m * P
                            last = three(AB[m % 4][:, :], w_hi[:, u.slot, c:c + P], w_lo[:, u.slot, c:c + P],
                                         y_hi[:, 2 * half + t, :], y_lo[:, 2 * half + t, :], t == 0, t == 1)
                        last.then_inc(tiles_done, 1)

                gate(unit(l, base), q0, True)
                begin(unit(l, base + 1))
                up(unit(l, base + 1), q0, 0)
                up(unit(l, base + 1), q0, 1)
                with pe.Fori(0, PAIRS) as i:
                    for j in (0, 1):
                        at = lambda k: unit(l, base + 2 + 3 * j + k, i, 6, 24)
                        q = q0 + 2 * i + j
                        gate(at(0), q + 1)
                        begin(at(1))
                        up(at(1), q + 1, 0)
                        up(at(1), q + 1, 1)
                        down(at(2), q, j)
                down(unit(l, base + 32), q0 + GROUPS - 1, 0)

            def dil_scores(H, b):
                if b == 0:
                    pe.wait_ge(k_scaled, 3 * H + 3)
                else:
                    pe.wait_ge(dil_biased, 12 * H + 3 * b + FREE)
                    pe.wait_ge(dil_t_dve, 4 * H + b + FREE)
                t = slice(b * P, (b + 1) * P)
                pe.matmul(AB[0][:, :], xs[:, 0, t], xs[:, 1, :], start=True, stop=True)
                pe.matmul(AB[1][:, 0:P], xs[:, 2, t], xs[:, 3, t], start=True, stop=True)
                pe.matmul(AB[1][:, P:2 * P], xs[:, 4, t], xs[:, 5, t], start=True, stop=True).then_inc(dil_s, 1)

            def dil_turn(H, b):
                pe.wait_ge(dil_p, 4 * H + b + 1)
                if b:
                    pe.wait_ge(dil_t_act, 4 * H + b)
                for c in range(4):
                    pe.transpose(AB[2][:, c * P:(c + 1) * P], s_sb[:, c * P:(c + 1) * P], ident[:, :])
                for c in (4, 5):
                    last = pe.transpose(AB[1][:, (c - 2) * P:(c - 1) * P], s_sb[:, c * P:(c + 1) * P], ident[:, :])
                last.then_inc(dil_t, 1)

            def dil_values(H, b):
                if b == 0:
                    pe.wait_ge(v01_ready, 4 * H + 4 + 4)
                    pe.wait_ge(v2_ready, H + 1)
                    pe.wait_ge(ret_y, 4 * H + 2)
                pe.wait_ge(dil_t_act, 4 * H + b + 1)
                pe.wait_ge(dil_t_dve, 4 * H + b + 1 + FREE)
                o = AB[3][:, b * P:(b + 1) * P]
                for a in range(NB):
                    pe.matmul(o, dil_v[:, 0, a, :], p_t[:, a * P:(a + 1) * P], start=a == 0, stop=False)
                pe.matmul(o, dil_v[:, 1, b, :], p_t[:, 4 * P:5 * P], start=False, stop=False)
                pe.matmul(o, dil_v[:, 2, b, :], p_t[:, 5 * P:6 * P], start=False, stop=True).then_inc(dil_pv, 1)

            def ret_scores(H, n, a):
                if a == 0:
                    pe.wait_ge(ret_qk_lo, 2 * H + 2)
                    pe.wait_ge(dil_biased, 12 * H + FREE)
                else:
                    pe.wait_ge(ret_p, 4 * H + a + FREE)
                t = slice(a * P, (a + 1) * P)
                three(AB[0][:, :], k_hi[:, t], k_lo[:, t], q_split(y_hi_flat, n), q_split(y_lo_flat, n), True, True).then_inc(ret_s, 1)

            def ret_values(H, n, a):
                if a == 0:
                    pe.wait_ge(ret_v_lo_ready, 2 * H + 2)
                    pe.wait_ge(dil_lo, H + FREE)
                pe.wait_ge(ret_pt_lo, 4 * H + a + 1)
                for e in (0, 1):
                    c = (a % 2) * RET_DV + e * P
                    last = three(AB[2 + e][:, :], ret_v_hi[:, a, e * P:(e + 1) * P], v_lo[a // 2][:, c:c + P],
                                 pt_split(y_hi_flat, n, a), pt_split(y_lo_flat, n, a), a == 0, a == NB - 1)
                last.then_inc(ret_pv, 1)

            def qk_sums(H, i):
                if i == 0:
                    pe.wait_ge(dil_t_dve, 4 * H + FREE)
                pe.wait_ge(qk_squared, 6 * H + i + 1)
                for b in range(NB):
                    last = pe.matmul(AB[1][:, 4 * i + b:4 * i + b + 1], qk_sq[i % 2][:, b * P:(b + 1) * P], ones[:, 0:1],
                                     start=True, stop=True)
                last.then_inc(qk_sum, 1)

            def k_spread(H, g, bank):
                spread(bank, lambda b: rqk[:, (2 * g + 1) * NB + b:(2 * g + 1) * NB + b + 1]).then_inc(k_bcast, 1)

            def heads(l, n, prev, first=None):
                H = 4 * l + n
                at = lambda k: unit(l, HEAD_BASE + k, n, 8, 19)
                u = at(0)
                begin(u)
                pe.wait_ge(v01_ready, 4 * H + 2)
                tile_cols(u, PB[0], 0, first)
                if first is not None:
                    norm_sums(first)
                if prev:
                    dil_scores(H - 1, 0)
                pe.wait_ge(v01_ready, 4 * H + 3)
                tile_cols(u, PB[1], 1)
                if prev:
                    dil_turn(H - 1, 0)
                if first is not None:
                    norm_spread(first)
                u = at(1)
                begin(u)
                pe.wait_ge(v01_ready, 4 * H + 4)
                tile_tokens(u, PB[2], 0)
                if prev:
                    dil_values(H - 1, 0)
                    dil_scores(H - 1, 1)
                tile_tokens(u, PB[3], 1)
                pe.wait_ge(rope_step, 6 * H + 1)
                tile_tokens(u, PB[0], 2)
                if prev:
                    dil_turn(H - 1, 1)
                pe.wait_ge(rope_step, 6 * H + 4)
                tile_tokens(u, PB[1], 3)
                if prev:
                    dil_values(H - 1, 1)
                    dil_scores(H - 1, 2)
                u = at(2)
                begin(u)
                pe.wait_ge(ret_v_ready, 4 * H + 1)
                tile_cols(u, PB[2], 0)
                if prev:
                    dil_turn(H - 1, 2)
                pe.wait_ge(ret_v_ready, 4 * H + 2)
                tile_cols(u, PB[3], 1)
                if prev:
                    dil_values(H - 1, 2)
                    dil_scores(H - 1, 3)
                u = at(3)
                begin(u)
                pe.wait_ge(ret_v_ready, 4 * H + 3)
                tile_cols(u, PB[0], 0)
                if prev:
                    dil_turn(H - 1, 3)
                pe.wait_ge(ret_v_ready, 4 * H + 4)
                tile_cols(u, PB[1], 1)
                if prev:
                    dil_values(H - 1, 3)
                ret_scores(H, n, 0)
                u = at(4)
                begin(u)
                pe.wait_ge(rg_scaled, 2 * H + 1)
                tile_cols(u, PB[2], 0)
                qk_sums(H, 0)
                ret_scores(H, n, 1)
                ret_values(H, n, 0)
                pe.wait_ge(rg_scaled, 2 * H + 2)
                tile_cols(u, PB[3], 1)
                qk_sums(H, 1)
                ret_scores(H, n, 2)
                ret_values(H, n, 1)
                u = at(5)
                begin(u)
                pe.wait_ge(qk_squared, 6 * H + 1)
                tile_cols(u, PB[0], 0)
                qk_sums(H, 2)
                ret_scores(H, n, 3)
                ret_values(H, n, 2)
                pe.wait_ge(qk_squared, 6 * H + 2)
                tile_cols(u, PB[1], 1)
                qk_sums(H, 3)
                ret_values(H, n, 3)
                u = at(6)
                begin(u)
                pe.wait_ge(qk_squared, 6 * H + 3)
                tile_cols(u, PB[2], 0, width=P)
                qk_sums(H, 4)
                u = at(7)
                begin(u)
                pe.wait_ge(qk_squared, 6 * H + 4)
                tile_tokens(u, PB[3], 0)
                qk_sums(H, 5)
                pe.wait_ge(ret_sq_added, H + 1)
                pe.wait_ge(ret_p, 4 * H + 4 + FREE)
                for b in range(NB):
                    last = pe.matmul(AB[0][:, b:b + 1], ret_sq[0][:, b * P:(b + 1) * P], ones[:, 0:1],
                                     start=True, stop=True)
                last.then_inc(ret_sum, 1)
                pe.wait_ge(qk_squared, 6 * H + 5)
                tile_tokens(u, PB[0], 1)
                pe.wait_ge(v2_scaled, H + 1)
                for b in range(NB):
                    last = pe.transpose(AB[2][:, b * P:(b + 1) * P], v2_t[:, b * P:(b + 1) * P], ident[:, :])
                last.then_inc(v2_turned, 1)
                pe.wait_ge(qk_squared, 6 * H + 6)
                tile_tokens(u, PB[1], 2)
                pe.wait_ge(ret_newton, 3 * H + 3)
                spread(AB[3], lambda b: t_r[:, b:b + 1]).then_inc(ret_bcast, 1)
                pe.wait_ge(qk_newton, 4 * H + 4)
                k_spread(H, 0, AB[1])
                tile_tokens(u, PB[2], 3)
                k_spread(H, 1, AB[0])
                pe.wait_ge(v2_ready, H + 1)
                k_spread(H, 2, AB[2])

            def merge(l):
                def gate(u, M, t, at=None, width=2 * P, between={}):
                    pe.wait_ge(mg_scaled, 2 * M + t + 1)
                    tile_cols(u, PB[t], t if at is None else at, width=width, between=between)

                def branch(u, M, t, k0, k1, col, between={}):
                    pe.wait_ge(mg_y, 2 * M + t + 1)
                    for k in range(k0, k1):
                        for step in between.get(k, ()):
                            step()
                        c = (k - col) * P
                        last = three(PB[2 + t][:, :], w_hi[:, u.slot, c:c + P], w_lo[:, u.slot, c:c + P],
                                     y_hi[:, k, :], y_lo[:, k, :], k == k0, k == k1 - 1)
                    last.then_inc(tiles_done, 1)

                def gates(u, M):
                    begin(u)
                    gate(u, M, 0)
                    gate(u, M, 1)

                def branches(u, M):
                    begin(u)
                    branch(u, M, 0, 0, 8, 0)
                    branch(u, M, 1, 8, 12, 0)

                def wout(u, M, half):
                    begin(u)
                    pe.wait_ge(mg_lo_ready, M + 1)
                    for m in range(KT):
                        pe.wait_ge(mix_x, 8 * M + m + 5)
                        c = m * P
                        three(AB[m % 4][:, :], w_hi[:, u.slot, c:c + P], w_lo[:, u.slot, c:c + P],
                              mg_hi[:, half, :], mg_lo[:, half, :], True, True).then_inc(tiles_done, 1)

                M0, H = KT * l, 4 * l + 3
                pe.wait_ge(v01_ready, 4 * 4 * (l + 1) + 4)
                turn = lambda b: lambda: dil_turn(H, b)
                values = lambda b: lambda: dil_values(H, b)
                scores = lambda b: lambda: dil_scores(H, b)
                u = unit(l, MERGE_BASE)
                begin(u)
                gate(u, M0, 0, between={3: [scores(0)]})
                gate(u, M0, 1, between={2: [turn(0)], 4: [values(0), scores(1)]})
                u = unit(l, MERGE_BASE + 1)
                begin(u)
                pe.wait_ge(ret_lo, 8 * (l + 1) + FREE)
                branch(u, M0, 0, 0, 8, 0, between={3: [turn(1)], 5: [values(1), scores(2)]})
                u = unit(l, MERGE_BASE + 2)
                begin(u)
                gate(u, M0 + 1, 0, 0, P, between={4: [turn(2)], 6: [values(2), scores(3)]})
                u = unit(l, MERGE_BASE + 3)
                begin(u)
                gate(u, M0 + 1, 1, 0, P, between={6: [turn(3)]})
                dil_values(H, 3)
                u = unit(l, MERGE_BASE + 4)
                begin(u)
                pe.wait_ge(dil_lo, 4 * (l + 1) + FREE)
                branch(u, M0, 1, 8, 12, 8)
                branches(unit(l, MERGE_BASE + 5), M0 + 1)
                wout(unit(l, MERGE_BASE + 6), M0, 0)
                with pe.Fori(0, 3) as i:
                    for j in (0, 1):
                        at = lambda k: unit(l, MERGE_BASE + 7 + 3 * j + k, i, 6, 24)
                        M = M0 + 2 * i + j + 1
                        gates(at(0), M + 1)
                        branches(at(1), M + 1)
                        wout(at(2), M, 1 - j)
                wout(unit(l, MERGE_BASE + 25), M0 + 7, 1)

            pe.sem_inc(tiles_done, FIRST_CREDIT)
            pe.sem_inc(dil_pv, FREE)
            pe.wait_ge(decay_in, 16 * (DEPTH + 1))
            pe.matmul(AB[1][0:56, 0:2], sel[:, :], dexp[:, :], start=True, stop=True).then_inc(dexp_t, 1)
            pe.wait_ge(bias_in, 16 * 2)
            pe.wait_ge(relb_one, 1)
            for c, bank in enumerate((PB[0], PB[1], PB[2], PB[3], AB[2])):
                w = min(512, NT * WD - 512 * c)
                pe.matmul(bank[0:12, 0:w], relb[:, :], onehot[:, 512 * c:512 * c + w], start=True, stop=True).then_inc(bias_mm, 1)
            pe.wait_ge(ident_in, 16)
            pe.wait_ge(params_in, 16 * 7 * DEPTH)
            pe.transpose(AB[0][:, 0:DEPTH * ROWS], prow, ident[0:DEPTH * ROWS, 0:DEPTH * ROWS]).then_inc(params_t, 1)
            for m in range(KT):
                if m % 4 == 0:
                    pe.wait_ge(x_in[m // 4], 16)
                if m < 4:
                    pe.wait_ge(bias_evicted, m + 1)
                else:
                    pe.wait_ge(ffn_x, m - 3)
                for r in range(NB):
                    last = pe.transpose(PB[m % 4][:, r * P:(r + 1) * P], x_tok[:, r, m * P:(m + 1) * P], ident[:, :])
                last.then_inc(x_transposed, 1)
            pe.wait_ge(ones_set, 1)
            pe.wait_ge(ffn_x, 8)
            with pe.Fori(0, DEPTH) as l:
                ffn(l, 0)
                heads(l, 0, False, 3 * l + 1)
                with pe.Fori(1, RET_HEADS) as n:
                    heads(l, n, True)
                merge(l)
                ffn(l, 1)
            for half, banks in enumerate((PB, AB)):
                pe.wait_ge(ffn_x, 8 + 8 * GROUPS * 2 * DEPTH - 4 * (1 - half))
                for r in range(NB):
                    for m in range(4):
                        last = pe.transpose(banks[r][:, m * P:(m + 1) * P], xs[:, 4 * half + m, r * P:(r + 1) * P], ident[:, :])
                    last.then_inc(out_turned, 1)

        @block.scalar
        def _(act):
            def split(u, n=2048):
                act.wait_ge(raw_landed[u.slot], 32 * (u.turn + 1))
                act.wait_ge(tiles_done, u.tile - u.before + FIRST_CREDIT)
                act.activation(w_hi[:, u.slot, 0:n], raw[:, u.slot, 0:n], ACT.Copy).then_inc(weights_hi, 1)

            def done(tile):
                act.wait_ge(tiles_done, tile + 1 + FIRST_CREDIT)

            def start_norm(N, k, x_ready):
                for m in range(KT):
                    act.wait_ge(*x_ready(m))
                    act.activation(h_hi[:, m, :], xs[:, m, :], ACT.Copy,
                                   scale=par[:, R_N[k] + m:R_N[k] + m + 1]).then_inc(h_hi_ready, 1)
                    if m >= 3:
                        act.wait_ge(ssq_added, (KT - 1) * N + m - 2)
                    act.activation(n_sq[m % 2] if m else ssq, xs[:, m, :], ACT.Square).then_inc(x_squared, 1)

            def norm_factor(N):
                act.wait_ge(norm_var, N + 1)
                act.activation(n_ln[:, :], n_var[:, :], ACT.Ln).then_inc(norm_ln, 1)
                act.wait_ge(norm_ln, N + 1)
                act.activation(n_exp[:, :], n_ln[:, :], ACT.Exp, scale=-0.5).then_inc(norm_exp, 1)

            def norm_copy(N):
                act.wait_ge(norm_bcast, N + 1)
                act.activation(r_b[:, :], AB[1][:, :], ACT.Copy).then_inc(r_ready, 1)

            def ffn(l, f):
                base, q0, N = FFN_BASE[f], (2 * l + f) * GROUPS, 3 * l + 2 * f

                def sigmoids(q):
                    for t in (0, 1):
                        act.wait_ge(gate_scaled, 2 * q + t + 1 + 2)
                        act.activation(sig[:, t, :], gate_s[:, t, :], ACT.Sigmoid).then_inc(sig_ready, 1)

                def hidden_his(q, half):
                    for t in (0, 1):
                        act.wait_ge(hidden_ready, 2 * q + t + 1)
                        act.activation(y_hi[:, 2 * half + t, :], hidden[:, t, :], ACT.Copy).then_inc(hid_hi, 1)

                split(unit(l, base + 1))
                norm_factor(N)
                norm_copy(N)
                sigmoids(q0)
                split(unit(l, base + 2))
                hidden_his(q0, 0)
                with act.Fori(0, PAIRS) as i:
                    for j in (0, 1):
                        at = lambda k: unit(l, base + 2 + 3 * j + k, i, 6, 24)
                        q = q0 + 2 * i + j
                        split(at(1))
                        sigmoids(q + 1)
                        split(at(2))
                        hidden_his(q + 1, 1 - j)
                        split(at(3))
                if f == 0:
                    split(unit(l, base + 33))

            def dil_exps(H, b):
                act.wait_ge(dil_max, 8 * H + 2 * b + 2)
                act.activation(s_sb, s_sb, ACT.Exp, bias=neg_max[:, 0:1], accum_out=den[:, 0:1]).then_inc(dil_exp, 1)

            def dil_copy(H, b):
                act.wait_ge(dil_t, 4 * H + b + 1)
                act.wait_ge(dil_pv, 4 * H + b + FREE)
                act.activation(p_t[:, 0:512], AB[2][:, :], ACT.Copy).then_inc(dil_t_act, 1)

            def dil_out(H, j):
                act.wait_ge(dil_pv, 4 * H + 4 + FREE)
                act.activation(y_hi[:, ds(8 + j, 1), :], AB[3][:, :].unsqueeze(1), ACT.Copy).then_inc(dil_hi, 1)

            def swap_halves(H, i, tile):
                done(tile)
                if i == 0:
                    act.wait_ge(ret_lo, 2 * H + FREE)
                else:
                    act.wait_ge(rope_step, 6 * H + 3)
                act.activation(swap[0:64, :], PB[i][64:128, :], ACT.Copy).then_inc(swapped, 1)
                act.activation(swap[64:128, :], PB[i][0:64, :], ACT.Copy).then_inc(swapped, 1)

            def rope_hi(H, n, i):
                act.wait_ge(rope_step, 6 * H + 3 * i + 3)
                act.activation(mg_hi[:, 1:2, :] if i else y_hi[:, ds(8 + n, 1), :], xs[:, 6 + i:7 + i, :], ACT.Copy).then_inc(ret_qk_hi, 1)

            def ret_values(H, b, tile, bank):
                done(tile)
                act.activation(ret_v[:, b, :], bank[:, 0:RET_DV], ACT.Copy, scale=r_col[:, b:b + 1]).then_inc(ret_v_ready, 1)

            def y_tile(n, e, parts, source):
                place = y_hi[:, :, :].rearrange("p t (h c) -> p (t h) c", h=parts)
                return (place[:, ds(2 * parts * n + parts * e, parts), :],
                        source.rearrange("p (h c) -> p h c", h=parts))

            def scores_hi(H, n, a):
                act.wait_ge(ret_p, 4 * H + a + 1 + FREE)
                if a >= 2:
                    act.wait_ge(ret_pv, 4 * H + a - 1)
                place, source = y_tile(n, a % 2, 1 + a // 2, ret_pt[a % 2])
                act.activation(place, source, ACT.Copy).then_inc(ret_pt_hi, 1)

            def qk_tile(H, i, tile, bank):
                done(tile)
                act.activation(xs[:, i, :], bank[:, :], ACT.Copy,
                               scale=gq[:, 0:1] if i % 2 == 0 else par[:, R_KN:R_KN + 1])
                if i >= 2:
                    act.wait_ge(qk_sum, 6 * H + i - 1)
                act.activation(qk_sq[i % 2], bank[:, :], ACT.Square).then_inc(qk_squared, 1)

            def v01(H, b, tile, bank):
                done(tile)
                act.activation(dil_v[:, 0:2, b, :], bank[:, 0:2 * P].rearrange("p (g n) -> p g n", g=2), ACT.Copy,
                               scale=r_col[:, b:b + 1]).then_inc(v01_ready, 1)

            def heads(l, n, prev, first=None):
                H = 4 * l + n
                at = lambda k: unit(l, HEAD_BASE + k, n, 8, 19)
                T = at(0).tile
                split(at(1))
                if first is not None:
                    norm_factor(first)
                    norm_copy(first)
                swap_halves(H, 0, T)
                if prev:
                    dil_exps(H - 1, 0)
                swap_halves(H, 1, T + 1)
                rope_hi(H, n, 0)
                if prev:
                    dil_copy(H - 1, 0)
                split(at(2))
                rope_hi(H, n, 1)
                ret_values(H, 0, T + 2, PB[2])
                if prev:
                    dil_exps(H - 1, 1)
                ret_values(H, 1, T + 3, PB[3])
                ret_values(H, 2, T + 4, PB[0])
                if prev:
                    dil_copy(H - 1, 1)
                ret_values(H, 3, T + 5, PB[1])
                if prev:
                    dil_exps(H - 1, 2)
                split(at(3))
                if prev:
                    dil_copy(H - 1, 2)
                    dil_exps(H - 1, 3)
                for e in (0, 1):
                    act.wait_ge(rope_step, 6 * H + 6)
                    act.wait_ge(rg_scaled, 2 * H + e + 1)
                    act.activation(work[:, 10 + e, :], silu[:, e, :], ACT.Sigmoid).then_inc(rg_sig, 1)
                if prev:
                    dil_copy(H - 1, 3)
                split(at(4))
                act.wait_ge(ret_v_ready, 4 * H + 4)
                act.activation(ret_v_hi[:, :, :], ret_v, ACT.Copy).then_inc(ret_v_hi_ready, 1)
                act.wait_ge(x_spilled, 16 * (l + 1))
                qk_tile(H, 0, T + 8, PB[0])
                if prev:
                    dil_out(H - 1, n - 1)
                qk_tile(H, 1, T + 9, PB[1])
                split(at(5))
                scores_hi(H, n, 0)
                qk_tile(H, 2, T + 10, PB[2])
                scores_hi(H, n, 1)
                qk_tile(H, 3, T + 11, PB[3])
                split(at(6), 1024)
                scores_hi(H, n, 2)
                qk_tile(H, 4, T + 12, PB[0])
                scores_hi(H, n, 3)
                qk_tile(H, 5, T + 13, PB[1])
                act.wait_ge(ret_pv, 4 * H + 4)
                for e in (0, 1):
                    act.activation(ret_sq[e], AB[2 + e][:, :], ACT.Square).then_inc(ret_o_read, 1)
                for e in (0, 1):
                    act.activation(ret_og[e], AB[2 + e][:, :], ACT.Copy,
                                   scale=par[:, ds(2 * n + R_RN + e, 1)]).then_inc(ret_o_read, 1)
                split(at(7))
                v01(H, 0, T + 15, PB[3])
                act.wait_ge(ret_var, H + 1)
                act.activation(t_ln[:, :], t_var[:, :], ACT.Ln).then_inc(ret_ln, 1)
                act.wait_ge(ret_ln, H + 1)
                act.activation(t_exp[:, :], t_ln[:, :], ACT.Exp, scale=-0.5).then_inc(ret_exp, 1)
                act.wait_ge(qk_var, 2 * H + 2)
                act.activation(q_ln[:, :], q_var[:, :], ACT.Ln).then_inc(qk_ln, 1)
                act.wait_ge(qk_ln, H + 1)
                act.activation(q_exp[:, :], q_ln[:, :], ACT.Exp, scale=-0.5).then_inc(qk_exp, 1)
                v01(H, 1, T + 16, PB[0])
                act.wait_ge(v2_turned, H + 1)
                act.activation(dil_v[:, 2, :, :].rearrange("p b n -> p (b n)"), AB[2][:, :], ACT.Copy).then_inc(v2_ready, 1)
                split(at(8))
                v01(H, 2, T + 17, PB[1])
                v01(H, 3, T + 18, PB[2])
                for e in (0, 1):
                    act.wait_ge(ret_y, 4 * H + 3 + e)
                    place, source = y_tile(n, e, 4, ret_og[e])
                    act.activation(place, source, ACT.Copy).then_inc(ret_hi, 1)

            def merge(l):
                def gate(M, m, t, half):
                    act.wait_ge(mg_scaled, 2 * M + t + 1 + 2)
                    act.activation(mg_sigm[half][:, t, :], mg_gate[half][:, t, :], ACT.Sigmoid,
                                   bias=par[:, ds(m + R_BG + KT * t, 1)]).then_inc(mg_sig, 1)

                def merged_hi(M, half):
                    act.wait_ge(mg_sum, M + 1)
                    act.activation(mg_hi[:, half, :], merged_t, ACT.Copy).then_inc(mg_hi_ready, 1)

                M0, H = KT * l, 4 * l + 3
                split(unit(l, MERGE_BASE + 1), 1024)
                dil_exps(H, 0)
                dil_copy(H, 0)
                dil_exps(H, 1)
                split(unit(l, MERGE_BASE + 2), 1024)
                dil_copy(H, 1)
                dil_exps(H, 2)
                split(unit(l, MERGE_BASE + 3), 1024)
                dil_copy(H, 2)
                dil_exps(H, 3)
                split(unit(l, MERGE_BASE + 4), 512)
                dil_copy(H, 3)
                dil_out(H, 3)
                split(unit(l, MERGE_BASE + 5), 1536)
                for t in (0, 1):
                    gate(M0, 0, t, 0)
                for t in (0, 1):
                    gate(M0 + 1, 1, t, 1)
                merged_hi(M0, 0)
                split(unit(l, MERGE_BASE + 6), 1024)
                split(unit(l, MERGE_BASE + 7))
                merged_hi(M0 + 1, 1)

                def blocks(i, j, n_next=2048):
                    at = lambda k: unit(l, MERGE_BASE + 7 + 3 * j + k, i, 6, 24)
                    M, m = M0 + 2 * i + j + 2, 2 * i + j + 2
                    split(at(1), 1536)
                    for t in (0, 1):
                        gate(M, m, t, j)
                    split(at(2), 1024)
                    split(at(3), n_next)
                    merged_hi(M, j)

                with act.Fori(0, 2) as i:
                    for j in (0, 1):
                        blocks(i, j)
                blocks(2, 0)
                blocks(2, 1, 1024)
                split(unit(l, MERGE_BASE + 26))

            act.sem_inc(v01_ready, 4)
            act.dma_start(ident[:, :], c_ident).then_inc(ident_in, 16)
            for c in (0, 1):
                act.dma_start(x_tok[:, :, c * 512:(c + 1) * 512],
                              x[0][:, c * 512:(c + 1) * 512].rearrange("(i r) d -> i r d", r=NB)).then_inc(x_in[c], 16)
            act.wait_ge(dstep, 1)
            act.activation(d_y[:, :], d_e[:, :], ACT.Exp, scale=-math.log(2.0)).then_inc(d_exp, 1)
            act.wait_ge(dstep, 2)
            act.activation(d_ln[:, :], d_w[:, :], ACT.Ln).then_inc(d_log, 1)
            act.wait_ge(d_log, 2)
            act.activation(dpos, dpos, ACT.Exp).then_inc(decay_done, 1)
            act.wait_ge(params_ready, 1)
            with act.Fori(0, DEPTH) as l:
                act.wait_ge(h_lo_ready, 24 * l + FREE)
                act.activation(par[:, :], params[:, ds(ROWS * l, ROWS)], ACT.Copy).then_inc(par_ready, 1)
                act.wait_ge(par_ready, 2 * l + 1)
                act.activation(gq[:, :], par[:, R_QN:R_QN + 1], ACT.Copy, scale=DIL_DH ** -0.5).then_inc(par_ready, 1)
                split(unit(l, 0))
                start_norm(3 * l, 0, lambda m: (ffn_x, 8 * GROUPS * 2 * l + m + 1))
                ffn(l, 0)
                start_norm(3 * l + 1, 1, lambda m: (ffn_x, 8 * GROUPS * (2 * l + 1) + m + 1))
                act.dma_start(x_spill, xs[:, :, :]).then_inc(x_spilled, 16)
                heads(l, 0, False, 3 * l + 1)
                with act.Fori(1, RET_HEADS) as n:
                    heads(l, n, True)
                merge(l)
                start_norm(3 * l + 2, 2, lambda m: (mix_x, 8 * KT * (l + 1) - KT + m + 1 + 8))
                ffn(l, 1)

        @block.vector
        def _(dve):
            def split(u, n=2048):
                dve.wait_ge(weights_hi, u.index + 1)
                dve.tensor_tensor(w_lo[:, u.slot, 0:n], raw[:, u.slot, 0:n], w_hi[:, u.slot, 0:n].bitcast(fp32),
                                  ALU.subtract).then_inc(weights_lo, 1)

            def done(tile):
                dve.wait_ge(tiles_done, tile + 1 + FIRST_CREDIT)

            def gained_lo(N, k, m):
                dve.wait_ge(h_hi_ready, 8 * N + m + 1)
                dve.scalar_tensor_tensor(h_lo[:, m, :], xs[:, m, :], par[:, R_N[k] + m:R_N[k] + m + 1],
                                         h_hi[:, m, :].bitcast(fp32), ALU.mult, ALU.subtract).then_inc(h_lo_ready, 1)

            def newton(y, y0, a, b, var, counter, at):
                dve.scalar_tensor_tensor(a[:, :], y0[:, :], -0.5, y0[:, :], ALU.mult, ALU.mult).then_inc(counter, 1)
                dve.wait_ge(counter, at + 1)
                dve.tensor_tensor(b[:, :], a[:, :], var[:, :], ALU.mult).then_inc(counter, 1)
                dve.wait_ge(counter, at + 2)
                dve.scalar_tensor_tensor(y[:, :], b[:, :], 1.5, y0[:, :], ALU.add, ALU.mult).then_inc(counter, 1)

            def norm_factor(N):
                dve.wait_ge(norm_sum, N + 1)
                dve.tensor_scalar(n_var[:, :], AB[0][:, 0:NB], 1.0 / D_MODEL, EPS, ALU.mult, ALU.add).then_inc(norm_var, 1)
                dve.wait_ge(norm_exp, N + 1)
                newton(r_col, n_exp, n_a, n_b, n_var, norm_newton, 3 * N)

            def ffn(l, f, norm_after):
                base, q0, N = FFN_BASE[f], (2 * l + f) * GROUPS, 3 * l + 2 * f

                def gates(u, q):
                    for t in (0, 1):
                        done(u.tile + t)
                        dve.tensor_tensor(gate_s[:, t, :], PB[t][:, :], r_b[:, :], ALU.mult).then_inc(gate_scaled, 1)
                    for t in (0, 1):
                        dve.wait_ge(sig_ready, 2 * q + t + 1)
                        dve.tensor_tensor(gated[:, t, :], gate_s[:, t, :], sig[:, t, :], ALU.mult).then_inc(gated_ready, 1)

                def ups(u, q, half):
                    for t in (0, 1):
                        done(u.tile + t)
                        dve.tensor_tensor(hidden[:, t, :], PB[2 + t][:, :], r_b[:, :], ALU.mult).then_inc(up_scaled, 1)
                        dve.wait_ge(up_scaled, 2 * q + t + 1 + 2)
                        dve.wait_ge(gated_ready, 2 * q + t + 1)
                        dve.tensor_tensor(hidden[:, t, :], hidden[:, t, :], gated[:, t, :], ALU.mult).then_inc(hidden_ready, 1)
                    for t in (0, 1):
                        dve.wait_ge(hid_hi, 2 * q + t + 1)
                        dve.tensor_tensor(y_lo[:, 2 * half + t, :], hidden[:, t, :], y_hi[:, 2 * half + t, :].bitcast(fp32),
                                          ALU.subtract).then_inc(hid_lo, 1)

                def add_down(u, q, m):
                    done(u.tile + m)
                    dve.wait_ge(ffn_x, 8 * q + m + 1)
                    dve.scalar_tensor_tensor(xs[:, m, :], AB[m % 4][:, :], 0.5, xs[:, m, :], ALU.mult, ALU.add).then_inc(ffn_x, 1)

                split(unit(l, base + 1))
                norm_factor(N)
                dve.wait_ge(r_ready, N + 1)
                gates(unit(l, base), q0)
                split(unit(l, base + 2))
                ups(unit(l, base + 1), q0, 0)
                with dve.Fori(0, PAIRS) as i:
                    for j in (0, 1):
                        at = lambda k: unit(l, base + 2 + 3 * j + k, i, 6, 24)
                        q = q0 + 2 * i + j
                        split(at(1))
                        gates(at(0), q + 1)
                        split(at(2))
                        ups(at(1), q + 1, 1 - j)
                        for m in range(KT):
                            if m == 4:
                                split(at(3))
                            add_down(at(2), q, m)
                if f == 0:
                    split(unit(l, base + 33))
                for m in range(KT):
                    add_down(unit(l, base + 32), q0 + GROUPS - 1, m)
                    if norm_after is not None and m:
                        gained_lo(norm_after, 1, m - 1)
                if norm_after is not None:
                    gained_lo(norm_after, 1, KT - 1)

            def dil_softmax(H, b):
                if b == 0:
                    dve.wait_ge(bias_landed, 16 * H + 16)
                dve.wait_ge(dil_s, 4 * H + b + 1)
                for g, (c, n, bank, at, off) in enumerate(((0, 4 * P, AB[0], 0, (3 - b) * P), (4 * P, P, AB[1], 0, NC * P),
                                                           (5 * P, P, AB[1], P, (NC + 1) * P))):
                    q = 2 * g * NB + b
                    dve.scalar_tensor_tensor(s_sb[:, c:c + n], bank[:, at:at + n], rqk[:, q:q + 1], bias_f[:, off:off + n],
                                             ALU.mult, ALU.add).then_inc(dil_biased, 1)
                dve.wait_ge(dil_biased, 12 * H + 3 * b + 3 + FREE)
                dve.tensor_reduce(row_max[:, :], s_sb, axis=AX.X, op=ALU.max).then_inc(dil_max, 1)
                dve.wait_ge(dil_max, 8 * H + 2 * b + 1)
                dve.tensor_scalar(neg_max[:, :], row_max[:, :], -1.0, None, ALU.mult).then_inc(dil_max, 1)

            def dil_divide(H, b):
                dve.wait_ge(dil_exp, 4 * H + b + 1)
                dve.reciprocal(rden[:, :], den[:, :]).then_inc(dil_recip, 1)
                dve.wait_ge(dil_recip, 4 * H + b + 1)
                dve.tensor_scalar(s_sb, s_sb, rden[:, 0:1], None, ALU.mult).then_inc(dil_p, 1)

            def dil_copy(H, b):
                dve.wait_ge(dil_t, 4 * H + b + 1)
                dve.wait_ge(dil_pv, 4 * H + b + FREE)
                dve.tensor_copy(p_t[:, 4 * P:6 * P], AB[1][:, 2 * P:4 * P]).then_inc(dil_t_dve, 1)

            def dil_out(H, j):
                dve.wait_ge(dil_hi, H + 1)
                dve.tensor_tensor(y_lo[:, ds(8 + j, 1), :], AB[3][:, :].unsqueeze(1),
                                  y_hi[:, ds(8 + j, 1), :].bitcast(fp32), ALU.subtract).then_inc(dil_lo, 1)

            def rope(H, i):
                dve.wait_ge(swapped, 4 * H + 2 * i + 2)
                dve.tensor_tensor(rope_c, PB[i][:, :], cos_r[:, :], ALU.mult).then_inc(rope_step, 1)
                dve.tensor_tensor(swap, swap, sin_r[:, :], ALU.mult).then_inc(rope_step, 1)
                dve.wait_ge(rope_step, 6 * H + 3 * i + 2)
                dve.tensor_tensor(xs[:, 6 + i, :], rope_c, swap, ALU.add).then_inc(rope_step, 1)

            def rope_lo(H, n, i):
                hi, lo = (k_hi, k_lo) if i else (q_split(y_hi_flat, n), q_split(y_lo_flat, n))
                dve.wait_ge(ret_qk_hi, 2 * H + i + 1)
                dve.tensor_tensor(lo, xs[:, 6 + i, :], hi.bitcast(fp32), ALU.subtract).then_inc(ret_qk_lo, 1)

            def ret_decay(H, a):
                dve.wait_ge(ret_s, 4 * H + a + 1)
                dve.scalar_tensor_tensor(ret_pt[a % 2], AB[0][:, :], RET_DK ** -0.5, decay_f[:, (3 - a) * P:(7 - a) * P],
                                         ALU.mult, ALU.mult).then_inc(ret_p, 1)

            def scores_lo(H, n, a):
                dve.wait_ge(ret_pt_hi, 4 * H + a + 1)
                dve.tensor_tensor(pt_split(y_lo_flat, n, a), ret_pt[a % 2], pt_split(y_hi_flat, n, a).bitcast(fp32),
                                  ALU.subtract).then_inc(ret_pt_lo, 1)

            def heads(l, n, prev, first=None):
                H = 4 * l + n
                at = lambda k: unit(l, HEAD_BASE + k, n, 8, 19)
                T = at(0).tile
                split(at(1))
                if first is not None:
                    norm_factor(first)
                    dve.wait_ge(norm_newton, 3 * first + 3)
                    dve.tensor_copy(r6[:, :].rearrange("p (t b) -> p t b", b=NB),
                                    r_col[:, :].unsqueeze(1).to_broadcast([P, 6, NB])).then_inc(r6_ready, 1)
                    dve.wait_ge(r6_ready, 2 * l + 1)
                    dve.tensor_tensor(rr6[:, :], r6[:, :], r6[:, :], ALU.mult).then_inc(r6_ready, 1)
                    dve.wait_ge(r_ready, first + 1)
                    dve.wait_ge(rope_in, 32 * (l + 1))
                    dve.tensor_tensor(cos_r[:, :], cos_r[:, :], r_b[:, :], ALU.mult).then_inc(rope_tables, 1)
                    dve.tensor_tensor(sin_r[:, :], sin_r[:, :], r_b[:, :], ALU.mult).then_inc(rope_tables, 1)
                    dve.wait_ge(rope_tables, 2 * l + 2)
                    dve.wait_ge(x_spilled, 16 * (l + 1))
                rope(H, 0)
                if prev:
                    dil_softmax(H - 1, 0)
                    dil_divide(H - 1, 0)
                rope(H, 1)
                if prev:
                    dil_copy(H - 1, 0)
                split(at(2))
                if prev:
                    dil_softmax(H - 1, 1)
                    dil_divide(H - 1, 1)
                    dil_copy(H - 1, 1)
                rope_lo(H, n, 0)
                rope_lo(H, n, 1)
                if prev:
                    dil_softmax(H - 1, 2)
                    dil_divide(H - 1, 2)
                split(at(3))
                done(T + 6)
                dve.tensor_tensor(silu[:, 0, :], PB[2][:, :], r_b[:, :], ALU.mult).then_inc(rg_scaled, 1)
                if prev:
                    dil_copy(H - 1, 2)
                done(T + 7)
                dve.tensor_tensor(silu[:, 1, :], PB[3][:, :], r_b[:, :], ALU.mult).then_inc(rg_scaled, 1)
                if prev:
                    dil_softmax(H - 1, 3)
                    dil_divide(H - 1, 3)
                for e in (0, 1):
                    dve.wait_ge(rg_sig, 2 * H + e + 1)
                    dve.tensor_tensor(silu[:, e, :], silu[:, e, :], work[:, 10 + e, :], ALU.mult).then_inc(silu_ready, 1)
                if prev:
                    dil_copy(H - 1, 3)
                split(at(4))
                if prev:
                    dil_out(H - 1, n - 1)
                dve.wait_ge(ret_v_hi_ready, H + 1)
                for a in (0, 2):
                    dve.tensor_tensor(v_lo[a // 2], work[:, a // 2, :],
                                      ret_v_hi[:, a:a + 2, :].rearrange("p b n -> p (b n)").bitcast(fp32),
                                      ALU.subtract).then_inc(ret_v_lo_ready, 1)
                dve.wait_ge(decay_landed, 16 * H + 16)
                ret_decay(H, 0)
                split(at(5))
                scores_lo(H, n, 0)
                ret_decay(H, 1)
                scores_lo(H, n, 1)
                ret_decay(H, 2)
                split(at(6), 1024)
                scores_lo(H, n, 2)
                ret_decay(H, 3)
                scores_lo(H, n, 3)
                split(at(7))
                done(T + 14)
                dve.tensor_tensor(v2_t, PB[2][:, :], r_b[:, :], ALU.mult).then_inc(v2_scaled, 1)
                dve.wait_ge(ret_sum, H + 1)
                dve.tensor_scalar(t_var[:, :], AB[0][:, 0:NB], 1.0 / RET_DV, EPS, ALU.mult, ALU.add).then_inc(ret_var, 1)
                dve.wait_ge(qk_sum, 6 * H + 6)
                dve.wait_ge(r6_ready, 2 * l + 2)
                dve.scalar_tensor_tensor(q_raw[:, :], AB[1][:, 0:NQ], 1.0 / DIL_DH, rr6[:, :], ALU.mult, ALU.mult).then_inc(qk_var, 1)
                dve.wait_ge(qk_var, 2 * H + 1)
                dve.tensor_scalar(q_var[:, :], q_raw[:, :], EPS, None, ALU.add).then_inc(qk_var, 1)
                dve.wait_ge(ret_exp, H + 1)
                newton(t_r, t_exp, t_a, t_b, t_var, ret_newton, 3 * H)
                dve.wait_ge(qk_exp, H + 1)
                newton(q_y, q_exp, q_a, q_b, q_var, qk_newton, 4 * H)
                dve.wait_ge(qk_newton, 4 * H + 3)
                dve.tensor_tensor(rqk[:, :], q_y[:, :], r6[:, :], ALU.mult).then_inc(qk_newton, 1)
                split(at(8))
                dve.wait_ge(ret_bcast, H + 1)
                for e in (0, 1):
                    dve.tensor_tensor(ret_og[e], ret_og[e], AB[3][:, :], ALU.mult).then_inc(ret_y, 1)
                for e in (0, 1):
                    dve.wait_ge(ret_y, 4 * H + 1 + e)
                    dve.tensor_tensor(ret_og[e], ret_og[e], silu[:, e, :], ALU.mult).then_inc(ret_y, 1)
                for g, bank in enumerate((AB[1], AB[0], AB[2])):
                    dve.wait_ge(k_bcast, 3 * H + g + 1)
                    dve.tensor_tensor(xs[:, 2 * g + 1, :], xs[:, 2 * g + 1, :], bank[:, :], ALU.mult).then_inc(k_scaled, 1)
                for e in (0, 1):
                    dve.wait_ge(ret_hi, 2 * H + e + 1)
                    dve.tensor_tensor(y_lo[:, ds(2 * n + e, 1), :], ret_og[e].unsqueeze(1),
                                      y_hi[:, ds(2 * n + e, 1), :].bitcast(fp32), ALU.subtract).then_inc(ret_lo, 1)

            def merge(l):
                def gate(tile, t, half):
                    done(tile)
                    dve.tensor_tensor(mg_gate[half][:, t, :], PB[t][:, :], r_b[:, :], ALU.mult).then_inc(mg_scaled, 1)

                def merged(tile0, tile1, M, half):
                    for t, tile in enumerate((tile0, tile1)):
                        done(tile)
                        dve.wait_ge(mg_sig, 2 * M + t + 1)
                        dve.tensor_tensor(mg_prod[:, t, :], PB[2 + t][:, :], mg_sigm[half][:, t, :], ALU.mult).then_inc(mg_y, 1)
                    dve.wait_ge(mg_y, 2 * M + 2 + 2)
                    dve.tensor_tensor(merged_t, mg_prod[:, 0, :], mg_prod[:, 1, :], ALU.add).then_inc(mg_sum, 1)
                    dve.wait_ge(mg_hi_ready, M + 1)
                    dve.tensor_tensor(mg_lo[:, half, :], merged_t, mg_hi[:, half, :].bitcast(fp32), ALU.subtract).then_inc(mg_lo_ready, 1)

                def add_out(u, M, m):
                    done(u.tile + m)
                    dve.wait_ge(mix_x, 8 * M + m + 1)
                    dve.tensor_tensor(xs[:, m, :], AB[m % 4][:, :], xs[:, m, :], ALU.add).then_inc(mix_x, 1)

                M0, H = KT * l, 4 * l + 3
                T = unit(l, MERGE_BASE).tile
                split(unit(l, MERGE_BASE + 1), 1024)
                dil_softmax(H, 0)
                dil_divide(H, 0)
                gate(T, 0, 0)
                dil_copy(H, 0)
                dil_softmax(H, 1)
                dil_divide(H, 1)
                gate(T + 1, 1, 0)
                split(unit(l, MERGE_BASE + 2), 1024)
                dil_copy(H, 1)
                dil_softmax(H, 2)
                dil_divide(H, 2)
                split(unit(l, MERGE_BASE + 3), 1024)
                dil_copy(H, 2)
                dil_softmax(H, 3)
                gate(T + 3, 0, 1)
                dil_divide(H, 3)
                split(unit(l, MERGE_BASE + 4), 512)
                dil_copy(H, 3)
                dil_out(H, 3)
                split(unit(l, MERGE_BASE + 5), 1536)
                gate(T + 4, 1, 1)
                merged(T + 2, T + 5, M0, 0)
                split(unit(l, MERGE_BASE + 6), 1024)
                dve.wait_ge(x_restored, 16 * (l + 1))
                for m in range(KT):
                    if m == 4:
                        split(unit(l, MERGE_BASE + 7))
                        merged(T + 6, T + 7, M0 + 1, 1)
                    add_out(unit(l, MERGE_BASE + 6), M0, m)

                def blocks(i, j, last=False):
                    at = lambda k: unit(l, MERGE_BASE + 7 + 3 * j + k, i, 6, 24)
                    M = M0 + 2 * i + j + 1
                    split(at(1), 1536)
                    for t in (0, 1):
                        gate(at(0).tile + t, t, j)
                    split(at(2), 1024)
                    if last:
                        merged(at(1).tile, at(1).tile + 1, M + 1, j)
                    for m in range(KT):
                        if m == 4:
                            split(at(3), 1024 if last else 2048)
                            if not last:
                                merged(at(1).tile, at(1).tile + 1, M + 1, j)
                        add_out(at(2), M, m)

                with dve.Fori(0, 2) as i:
                    for j in (0, 1):
                        blocks(i, j)
                blocks(2, 0)
                blocks(2, 1, last=True)
                split(unit(l, MERGE_BASE + 26))
                for m in range(KT):
                    add_out(unit(l, MERGE_BASE + 25), M0 + 7, m)
                    if m:
                        gained_lo(3 * l + 2, 2, m - 1)
                gained_lo(3 * l + 2, 2, KT - 1)

            dve.sem_inc(weights_lo, LO_CREDIT)
            for s in (gate_scaled, up_scaled, mg_scaled, mg_y):
                dve.sem_inc(s, 2)
            for s in (ret_p, dil_biased, ret_lo, dil_t_dve, dil_lo, h_lo_ready):
                dve.sem_inc(s, FREE)
            dve.sem_inc(mix_x, 8)
            dve.memset(ones[:, :], 1.0).then_inc(ones_set, 1)
            dve.memset(relb[N_BUCKETS:N_BUCKETS + 1, :], 1.0).then_inc(relb_one, 1)
            dve.wait_ge(dexp_t, 1)
            dve.tensor_copy(d_e[:, :], AB[1][0:56, 0:2]).then_inc(dstep, 1)
            steps = [2]

            def chain(ins):
                ins.then_inc(dstep, 1)
                dve.wait_ge(dstep, steps[0])
                steps[0] += 1

            dve.wait_ge(d_exp, 1)
            chain(dve.tensor_scalar(d_w[:, :], d_y[:, :], -1.0, 1.0, ALU.mult, ALU.add))
            chain(dve.tensor_scalar(d_d[:, :], d_y[:, :], -1.0, 2.0, ALU.mult, ALU.add))
            chain(dve.reciprocal(d_d[:, :], d_d[:, :]))
            chain(dve.tensor_tensor(d_s[:, :], d_y[:, :], d_d[:, :], ALU.mult))
            chain(dve.tensor_tensor(d_s2[:, :], d_s[:, :], d_s[:, :], ALU.mult))
            chain(dve.tensor_scalar(d_p[:, :], d_s2[:, :], 1.0 / 19, None, ALU.mult))
            for odd in range(17, 1, -2):
                chain(dve.scalar_tensor_tensor(d_p[:, :], d_p[:, :], 1.0 / odd, d_s2[:, :], ALU.add, ALU.mult))
            chain(dve.scalar_tensor_tensor(d_p[:, :], d_p[:, :], 1.0, d_s[:, :], ALU.add, ALU.mult))
            chain(dve.tensor_scalar(d_lg[:, :], d_p[:, :], -2.0, None, ALU.mult))
            chain(dve.tensor_scalar(d_m[:, :], d_y[:, :], 0.5, None, ALU.is_gt))
            dve.wait_ge(d_log, 1)
            chain(dve.tensor_tensor(d_ln[:, :], d_ln[:, :], d_lg[:, :], ALU.subtract))
            chain(dve.tensor_tensor(d_ln[:, :], d_ln[:, :], d_m[:, :], ALU.mult))
            chain(dve.tensor_tensor(d_lg[:, :], d_lg[:, :], d_ln[:, :], ALU.add))
            dve.wait_ge(dist_in, 16)
            chain(dve.tensor_scalar(dpos, dist, 0.0, d_lg[:, 0:1], ALU.max, ALU.mult))
            chain(dve.tensor_scalar(dneg, dist, 0.0, d_lg[:, 1:2], ALU.min, ALU.mult))
            dve.tensor_tensor(dpos, dpos, dneg, ALU.subtract).then_inc(d_log, 1)
            for c, bank in enumerate((PB[0], PB[1], PB[2], PB[3], AB[2])):
                w = min(512, NT * WD - 512 * c)
                dve.wait_ge(bias_mm, c + 1)
                dve.tensor_copy(bdiag[c][:, 0:w], bank[0:12, 0:w]).then_inc(bias_evicted, 1)
            dve.wait_ge(params_t, 1)
            dve.tensor_copy(params[:, :], AB[0][:, 0:DEPTH * ROWS]).then_inc(params_ready, 1)
            for m in range(KT):
                dve.wait_ge(x_transposed, m + 1)
                dve.tensor_copy(xs[:, m, :], PB[m % 4][:, :]).then_inc(ffn_x, 1)
            with dve.Fori(0, DEPTH) as l:
                split(unit(l, 0))
                dve.wait_ge(par_ready, 2 * l + 2)
                for m in range(KT):
                    gained_lo(3 * l, 0, m)
                ffn(l, 0, 3 * l + 1)
                heads(l, 0, False, 3 * l + 1)
                with dve.Fori(1, RET_HEADS) as n:
                    heads(l, n, True)
                merge(l)
                ffn(l, 1, None)
            for n in range(8):
                dve.wait_ge(out_turned, n + 1)
                half, r = divmod(n, NB)
                dve.tensor_copy(x_tok[:, r, half * 512:half * 512 + 512], (PB, AB)[half][r][:, :]).then_inc(out_copied, 1)


def rope_tables():
    half = RET_DK // 2
    inv = np.float32(10000.0) ** (-np.arange(half, dtype=np.float32) / np.float32(half))
    tau = np.arange(SEQ)
    t = (4 * (tau % P) + tau // P).astype(np.float32)
    ang = (t[None, :] * inv.astype(np.float32)[:, None]).astype(np.float32)
    cos, sin = np.cos(ang).astype(np.float32), np.sin(ang).astype(np.float32)
    return np.concatenate([cos, cos]), np.concatenate([-sin, sin])


def bias_selection():
    sel = np.zeros((N_BUCKETS + 1, NT, WD), np.float32)
    nb = N_BUCKETS // 2
    for c in range(NT):
        for w in range(WD):
            step = w - (P - 1)
            rel = 4 * step + (c - 3 if c < NC else 0)
            valid = (abs(rel) <= 64, abs(step) <= 64, step % 4 == 0)[0 if c < NC else c - NC + 1]
            n = abs(rel)
            if n >= nb // 2:
                exact = nb // 2
                big = exact + int(np.float32(np.log(np.float32(n) / np.float32(exact))) / np.float32(math.log(MAX_DISTANCE / exact))
                                  * np.float32(nb - exact))
                n = min(big, nb - 1)
            sel[(nb if rel > 0 else 0) + n, c, w] = 1.0
            sel[N_BUCKETS, c, w] = 0.0 if valid else NEG
    return sel.reshape(N_BUCKETS + 1, NT * WD)


def token_distances():
    w = np.arange(WD)[None, :] - (P - 1)
    d = (4 * w + (np.arange(NC)[:, None] - 3)).astype(np.float32)
    return np.tile(d, (DEPTH * RET_HEADS, 1))


def constants():
    cos, sin = rope_tables()
    return {"c_ident": np.eye(P, dtype=np.float32), "c_cos": cos, "c_sin": sin, "c_onehot": bias_selection(),
            "c_dist": token_distances(), "c_sel": np.repeat(np.eye(DEPTH * RET_HEADS, dtype=np.float32), NC, axis=1)}


_INS = ["x", "rel_bias", "norm_ffn1", "ffn1_gate", "ffn1_up", "ffn1_down", "norm_mix", "w_in", "b_gate", "ret_decay_exp",
        "ret_norm", "w_ret_o", "dil_q_norm", "dil_k_norm", "w_dil_o", "w_out", "norm_ffn2", "ffn2_gate", "ffn2_up",
        "ffn2_down"]


def kernel(**inputs):
    import concourse.bacc as bacc
    from concourse.bass_utils import run_bass_kernel_spmd

    nc = bacc.Bacc("TRN2", target_bir_lowering=False, num_devices=1)
    arrays = {f"in_{k}": np.ascontiguousarray(inputs[k]) for k in _INS}
    arrays.update(constants())
    args = {k.removeprefix("in_"): nc.dram_tensor(k, a.shape, mybir.dt.from_np(a.dtype), kind="ExternalInput").ap()
            for k, a in arrays.items()}
    out = nc.dram_tensor("out", (SEQ, D_MODEL), mybir.dt.float32, kind="ExternalOutput").ap()
    build(nc, out=out, **args)
    r = run_bass_kernel_spmd(nc, [arrays], core_ids=[0])
    return r.results[0]["out"].reshape(1, SEQ, D_MODEL)
```
